# Optimizing a Trainium2 kernel written in Bass

```python
import math
import jax, jax.numpy as jnp
from jax import lax
import numpy as np

D_MODEL = 1024
BATCH = 1
SEQ = 512
DEPTH = 1

CHUNK = 64
MIX_WIDTH = D_MODEL
RET_HEADS = 4
RET_VWIDTH = MIX_WIDTH // 2
RET_DV = RET_VWIDTH // RET_HEADS
RET_DK = RET_DV // 2
RET_QKWIDTH = RET_HEADS * RET_DK
POOL_WIDTH = MIX_WIDTH - RET_VWIDTH
POOL_WINDOWS = (2, 4, 8, 16)
POOL_GROUPS = len(POOL_WINDOWS)
POOL_GC = POOL_WIDTH // POOL_GROUPS
IN_WIDTH = 2 * RET_QKWIDTH + 2 * RET_VWIDTH + POOL_WIDTH
D_FF = 2816
ROPE_BASE = 10000.0
RMS_EPS = 1e-6
GN_EPS = 1e-5

kernel_name = "hybrid_retention_multiscale_pool_macaron"

def rms_norm(x, g):
    xf = x.astype(jnp.float32)
    y = xf * lax.rsqrt(jnp.mean(xf * xf, axis=-1, keepdims=True) + RMS_EPS)
    return (y * g.astype(jnp.float32)).astype(x.dtype)

def swiglu(x, w_gate, w_up, w_down):
    return (jax.nn.silu(x @ w_gate) * (x @ w_up)) @ w_down

def rotary(x, pos):
    d = x.shape[-1]
    half = d // 2
    freqs = ROPE_BASE ** (-jnp.arange(half, dtype=jnp.float32) * 2.0 / d)
    ang = pos.astype(jnp.float32)[:, None] * freqs[None, :]
    cos = jnp.cos(ang)[None, :, None, :].astype(x.dtype)
    sin = jnp.sin(ang)[None, :, None, :].astype(x.dtype)
    x1, x2 = x[..., :half], x[..., half:]
    return jnp.concatenate([x1 * cos - x2 * sin, x1 * sin + x2 * cos], axis=-1)

def retention_chunkwise(q, k, v):
    b, s, h, dk = q.shape
    dv = v.shape[-1]
    n = s // CHUNK
    dt = q.dtype
    gamma = 1.0 - 2.0 ** (-5.0 - jnp.arange(h, dtype=jnp.float32))
    log_g = jnp.log(gamma)
    idx = jnp.arange(CHUNK, dtype=jnp.float32)
    d_intra = jnp.exp(log_g[:, None, None] * jnp.abs(idx[:, None] - idx[None, :])).astype(dt)
    d_key = jnp.exp(log_g[:, None] * (CHUNK - 1.0 - idx)[None, :]).astype(dt)
    d_query = jnp.exp(log_g[:, None] * (idx + 1.0)[None, :]).astype(dt)
    d_chunk = jnp.exp(log_g * CHUNK).astype(dt)

    qc = (q * (dk ** -0.5)).reshape(b, n, CHUNK, h, dk)
    kc = k.reshape(b, n, CHUNK, h, dk)
    vc = v.reshape(b, n, CHUNK, h, dv)

    scores = jnp.einsum('bnihd,bnjhd->bnhij', qc, kc) * d_intra[None, None]
    intra = jnp.einsum('bnhij,bnjhe->bnihe', scores, vc)

    kv = jnp.einsum('bnjhd,hj,bnjhe->nbhde', kc, d_key, vc)

    def step(state, kv_n):
        return state * d_chunk[None, :, None, None] + kv_n, state

    init = jnp.zeros((b, h, dk, dv), dtype=kv.dtype)
    _, s_prev = lax.scan(step, init, kv)
    cross = jnp.einsum('bnihd,nbhde,hi->bnihe', qc, s_prev, d_query)
    return (intra + cross).reshape(b, s, h, dv)

def head_group_norm(o, gain):
    b, s, h, dv = o.shape
    of = o.astype(jnp.float32)
    mu = jnp.mean(of, axis=-1, keepdims=True)
    var = jnp.mean(jnp.square(of - mu), axis=-1, keepdims=True)
    y = ((of - mu) * lax.rsqrt(var + GN_EPS)).reshape(b, s, h * dv)
    return (y * gain.astype(jnp.float32)).astype(o.dtype)

def multiscale_pool(u, w_pool, scale):
    b, s, _ = u.shape
    ug = u.reshape(b, s, POOL_GROUPS, POOL_GC)
    cs = jnp.cumsum(ug.astype(jnp.float32), axis=1)
    cs = jnp.concatenate([jnp.zeros((b, 1, POOL_GROUPS, POOL_GC), jnp.float32), cs], axis=1)
    t = jnp.arange(s)
    win = jnp.array(POOL_WINDOWS, dtype=jnp.int32)
    lo = jnp.maximum(t[:, None] + 1 - win[None, :], 0)
    cnt = (t[:, None] + 1 - lo).astype(jnp.float32)
    cs_lo = cs[:, lo, jnp.arange(POOL_GROUPS)[None, :], :]
    mean = (cs[:, 1:] - cs_lo) / cnt[None, :, :, None]
    pooled = mean.astype(u.dtype) - ug
    y = jnp.einsum('bsgc,gcd->bsgd', pooled, w_pool).reshape(b, s, POOL_WIDTH)
    return y * scale

def hybrid_mixer(h, w_in, w_out, ret_gn_gain, pool_w, pool_scale):
    b, s, _ = h.shape
    p = h @ w_in
    o1 = RET_QKWIDTH
    o2 = o1 + RET_QKWIDTH
    o3 = o2 + RET_VWIDTH
    o4 = o3 + RET_VWIDTH
    q = p[..., :o1].reshape(b, s, RET_HEADS, RET_DK)
    k = p[..., o1:o2].reshape(b, s, RET_HEADS, RET_DK)
    v = p[..., o2:o3].reshape(b, s, RET_HEADS, RET_DV)
    g = p[..., o3:o4]
    u = p[..., o4:]
    pos = jnp.arange(s)
    q = rotary(q, pos)
    k = rotary(k, pos)
    ret = retention_chunkwise(q, k, v)
    ret = jax.nn.silu(g) * head_group_norm(ret, ret_gn_gain)
    pool = multiscale_pool(u, pool_w, pool_scale)
    return jnp.concatenate([ret, pool], axis=-1) @ w_out

def setup_inputs(seed: int = 0) -> dict:
    key = jax.random.key(seed)
    ks = jax.random.split(key, 20)
    f32 = jnp.float32
    nrm = lambda k_, shape, fan: jax.random.normal(k_, shape, f32) * (fan ** -0.5)
    gain = lambda k_, shape: 1.0 + 0.02 * jax.random.normal(k_, shape, f32)
    L = DEPTH
    return {
        "x": jax.random.normal(ks[0], (BATCH, SEQ, D_MODEL), f32),
        "norm_ffn1": gain(ks[1], (L, D_MODEL)),
        "ffn1_gate": nrm(ks[2], (L, D_MODEL, D_FF), D_MODEL),
        "ffn1_up": nrm(ks[3], (L, D_MODEL, D_FF), D_MODEL),
        "ffn1_down": nrm(ks[4], (L, D_FF, D_MODEL), D_FF),
        "norm_mix": gain(ks[5], (L, D_MODEL)),
        "w_in": nrm(ks[6], (L, D_MODEL, IN_WIDTH), D_MODEL),
        "ret_gn_gain": gain(ks[7], (L, RET_VWIDTH)),
        "pool_w": nrm(ks[8], (L, POOL_GROUPS, POOL_GC, POOL_GC), POOL_GC),
        "pool_scale": gain(ks[9], (L, POOL_WIDTH)),
        "w_out": nrm(ks[10], (L, MIX_WIDTH, D_MODEL), MIX_WIDTH),
        "norm_ffn2": gain(ks[11], (L, D_MODEL)),
        "ffn2_gate": nrm(ks[12], (L, D_MODEL, D_FF), D_MODEL),
        "ffn2_up": nrm(ks[13], (L, D_MODEL, D_FF), D_MODEL),
        "ffn2_down": nrm(ks[14], (L, D_FF, D_MODEL), D_FF),
        "norm_final": gain(ks[15], (D_MODEL,)),
    }

def reference(x, norm_ffn1, ffn1_gate, ffn1_up, ffn1_down, norm_mix, w_in,
              ret_gn_gain, pool_w, pool_scale, w_out, norm_ffn2, ffn2_gate,
              ffn2_up, ffn2_down, norm_final):
    for l in range(DEPTH):
        x = x + 0.5 * swiglu(rms_norm(x, norm_ffn1[l]), ffn1_gate[l], ffn1_up[l], ffn1_down[l])
        x = x + hybrid_mixer(rms_norm(x, norm_mix[l]), w_in[l], w_out[l],
                             ret_gn_gain[l], pool_w[l], pool_scale[l])
        x = x + 0.5 * swiglu(rms_norm(x, norm_ffn2[l]), ffn2_gate[l], ffn2_up[l], ffn2_down[l])
    return rms_norm(x, norm_final)


_drawn_inputs = setup_inputs


def setup_inputs(seed=0):
    import zlib

    import numpy as np

    out = dict(_drawn_inputs(seed))
    spreads = {}
    factors = {'norm_ffn1': 5.429,
     'norm_mix': 3.161,
     'ret_gn_gain': 8.0,
     'pool_scale': 5.895,
     'norm_ffn2': 8.0,
     'norm_final': 2.857}
    for name, (base, spread) in spreads.items():
        noise = np.random.default_rng([zlib.crc32(name.encode()), seed]).standard_normal(out[name].shape)
        drawn = base * np.exp(spread * noise) if base else spread * noise
        out[name] = __import__('jax').numpy.asarray(drawn.astype(out[name].dtype))
    for name, factor in factors.items():
        out[name] = (out[name] * factor).astype(out[name].dtype)
    return out
```

```python
from contextlib import ExitStack

import numpy as np

import concourse.bass as bass
from concourse import mybir

F32 = mybir.dt.float32
F32R = mybir.dt.float32r
ACT = mybir.ActivationFunctionType
ALU = mybir.AluOpType

P = 128
D = 1024
T = 512
FF = 2816
KD = D // P
KF = FF // P
TT = T // P
HEADS = 4
DK = 64
DV = 128
CHUNK = 64
WINDOWS = (2, 4, 8, 16)
RMS_EPS = 1e-6
GN_EPS = 1e-5
ROPE_BASE = 10000.0

SLOTS = 4
UNIT = 1024
AHEAD = 2
DOWN_PARTS = ((0, 8), (8, 15), (15, 22))

GU_UNITS = 2 * KF
DOWN_UNITS = len(DOWN_PARTS) * KD
MIX_UNITS = 24
GU0 = (0, GU_UNITS + DOWN_UNITS + MIX_UNITS)
DOWN0 = (GU0[0] + GU_UNITS, GU0[1] + GU_UNITS)
MIX0 = DOWN0[0] + DOWN_UNITS
ALL_UNITS = DOWN0[1] + DOWN_UNITS
QK0, V0, G0, U0, O0 = 0, 4, 8, 12, 16

GAIN_NORM = (0, 8, 16, 24)
GAIN_RET = 32
GAIN_POOL = 36
GAINS = 40

NORM_FFN = (0, 2)
NORM_MIX = 1
NORM_OUT = 3

SCORE_AT = ((4, 0), (5, 0), (6, 0), (5, 384))
PT_AT = (0, 512, 896, 1152)
PT = 1280
CAT_FIRST, CAT_NEXT, CAT_LAST = (7, 6, 5, 0, 1), (4, 2), (3,)
U_BANK = (7, 4, 5, 6)


Y_DVE = 5
NORM_BANK, TOK_BANK = 4, 5

CAT_EVENTS = ("y0", "y1", "t0", "y2", "t1", "t2", "y3", "t3")
CAT_AFTER = ((), ("y0",), ("y1", "t0"), ("y2", "t1"))
RET_TASKS = (
    (("u", 0), ("stats", 0), ("norm", 0), ("mean", 0)),
    (("u", 1), ("stats", 1), ("norm", 1), ("mean", 1), ("cat", "y0")),
    (("u", 2), ("stats", 2), ("cat", "y1"), ("cat", "t0"), ("norm", 2), ("mean", 2)),
    (("u", 3), ("mean", 3), ("stats", 3), ("cat", "y2"), ("cat", "t1"), ("norm", 3),
     ("cat", "t2"), ("cat", "y3"), ("cat", "t3")),
)
SUM_STEPS = (0, 3, 5, 6)


def cat_place(event):
    n = int(event[1])
    if event[0] == "y":
        return U_BANK[n], HEADS + 3 - n, GAIN_POOL + 3 - n
    return n, n, GAIN_RET + n


def cat_count(k):
    return 1 + [cat_place(e)[1] for e in CAT_EVENTS].index(k)


def program(nc, xT, gate, up, down, gate2, up2, down2, w_qku, w_vg, w_out, pool_w, gains,
            decay, rope, edge, outT):
    with ExitStack() as ctx:
        def sb(name, shape, dt=F32, scope=ctx):
            return scope.enter_context(nc.sbuf_tensor(name, shape, dt))

        def sem(name):
            return ctx.enter_context(nc.semaphore(name))

        x = sb("x_sb", [P, KD, T])
        h_hi = sb("h_hi", [P, KD, T], F32R)
        h_lo = sb("h_lo", [P, KD, T], F32R)
        w_raw = sb("w_raw", [P, SLOTS, UNIT])
        w_hi = sb("w_hi", [P, SLOTS, UNIT], F32R)
        w_lo = sb("w_lo", [P, SLOTS, UNIT], F32R)
        rstd = sb("rstd", [P, 1, T])
        rms = sb("rms", [P, 1, T])
        ssq = sb("ssq", [P, 1, T])
        square = sb("square", [P, 2, T])
        tmp_a = sb("tmp_a", [P, 1, T])
        tmp_b = sb("tmp_b", [P, 1, T])
        gain = sb("gain", [P, GAINS])
        rope_sb = sb("rope_sb", [P, 2, T])
        mean_w = sb("mean_w", [P, P])
        eps = sb("eps", [P, 2])
        rms_tok = sb("rms_tok", [P, TT])
        rstd_tok = sb("rstd_tok", [P, TT])
        ident = sb("ident", [P, P])
        stats = sb("stats", [P, TT, 6])
        meanvar = sb("meanvar", [P, TT, 2])
        gn_std = sb("gn_std", [P, TT])
        gn_rstd = sb("gn_rstd", [P, TT])

        with ExitStack() as ffn_scope:
            a_hi = sb("a_hi", [P, KF, T], F32R, ffn_scope)
            a_lo = sb("a_lo", [P, KF, T], F32R, ffn_scope)
        with ExitStack() as mix_scope:
            qk = sb("qk", [P, 4, T], scope=mix_scope)
            v = sb("v", [P, TT, HEADS * DV], scope=mix_scope)
            pt = sb("pt", [P, HEADS, PT], scope=mix_scope)
            sg = sb("sg", [P, TT, HEADS * DV], scope=mix_scope)
            cat_hi = sb("cat_hi", [P, KD, T], F32R, mix_scope)
            cat_lo = sb("cat_lo", [P, KD, T], F32R, mix_scope)
            decay_sb = sb("decay_sb", [P, HEADS, T], scope=mix_scope)
            pool_w_sb = sb("pool_w_sb", [P, HEADS, P], scope=mix_scope)
            edge_sb = sb("edge_sb", [P, len(WINDOWS), 16], scope=mix_scope)
            rot_a = sb("rot_a", [P, 1, T], scope=mix_scope)
            rot_b = sb("rot_b", [P, 1, T], scope=mix_scope)
        u_sb = qk[:, 0:2, :]
        n_sb = qk[:, 2:4, :]

        ps = ctx.enter_context(nc.psum_tensor("ps", [P, 8, T], F32))

        raw_landed = [sem(f"raw_landed{s}") for s in range(SLOTS)]
        hi_split = sem("hi_split")
        lo_split = sem("lo_split")
        unit_done = sem("unit_done")
        x_landed = [sem(f"x_landed{k}") for k in range(KD)]
        gain_landed = sem("gain_landed")
        rope_landed = sem("rope_landed")
        mix_landed = sem("mix_landed")
        setup_step = sem("setup_step")
        setup_done = sem("setup_done")
        x_updated = sem("x_updated")
        h_hi_ready = sem("h_hi_ready")
        h_ready = sem("h_ready")
        square_ready = sem("square_ready")
        ssq_cleared = sem("ssq_cleared")
        ssq_added = sem("ssq_added")
        mean_done = sem("mean_done")
        rms_ready = sem("rms_ready")
        rstd_ready = sem("rstd_ready")
        tok_mean_done = sem("tok_mean_done")
        tok_rms_ready = sem("tok_rms_ready")
        tok_rstd_ready = sem("tok_rstd_ready")
        gate_scaled = sem("gate_scaled")
        up_scaled = sem("up_scaled")
        silu_ready = sem("silu_ready")
        a_ready = sem("a_ready")
        a_lo_ready = sem("a_lo_ready")
        rope_scaled = sem("rope_scaled")
        rot_ready = sem("rot_ready")
        qk_ready = sem("qk_ready")
        v_ready = sem("v_ready")
        sg_ready = sem("sg_ready")
        scores_done = sem("scores_done")
        pt_ready = sem("pt_ready")
        pv_done = sem("pv_done")
        u_ready = sem("u_ready")
        sum_step = sem("sum_step")
        sum_ready = sem("sum_ready")
        edge_done = sem("edge_done")
        pooled_ready = sem("pooled_ready")
        stats_ready = sem("stats_ready")
        var_ready = sem("var_ready")
        gn_std_ready = sem("gn_std_ready")
        gn_rstd_ready = sem("gn_rstd_ready")
        gn_scaled = sem("gn_scaled")
        ret_ready = sem("ret_ready")
        cat_done = sem("cat_done")
        cat_hi_ready = sem("cat_hi_ready")
        cat_ready = sem("cat_ready")
        final_gained = sem("final_gained")
        y_dve = sem("y_dve")
        y_pool = sem("y_pool")
        stored = sem("stored")

        def at(t, i):
            return t[:, bass.ds(i, 1), :]

        def known(n, least):
            return not (isinstance(n, int) and n < least)

        def rounds(n0):
            return n0 // SLOTS

        block = ctx.enter_context(nc.Block())

        @block.sync
        def _(sp):
            def load(rnd, c, src, width=UNIT):
                n, s = SLOTS * rnd + c, c % SLOTS
                if known(n, SLOTS):
                    sp.wait_ge(lo_split, n - SLOTS + 1)
                sp.dma_start(w_raw[:, s, 0:width], src).then_inc(raw_landed[s], 16)

            def load_gate_up(f, i):
                for c in range(4):
                    src = ((gate, up), (gate2, up2))[f][c % 2]
                    load(rounds(GU0[f]) + i, c,
                         src[bass.ds(2 * i + c // 2, 1), :, :].rearrange("a p c -> p (a c)"))

            def load_down(f, i):
                src = (down, down2)[f]
                for j in range(4):
                    for r, (k0, k1) in enumerate(DOWN_PARTS):
                        load(rounds(DOWN0[f]) + 3 * i, 3 * j + r,
                             src[bass.ds(4 * i + j, 1), :, k0 * P:k1 * P]
                             .rearrange("a p c -> p (a c)"), (k1 - k0) * P)

            load_gate_up(0, 0)
            with sp.Fori(1, KF // 2) as i:
                load_gate_up(0, i)
            with sp.Fori(0, 2) as i:
                load_down(0, i)
            units = ([w_qku[m] for m in range(4)] + [w_vg[m] for m in range(8)]
                     + [w_qku[7 - s] for s in range(4)] + [w_out[m] for m in range(KD)])
            for c, src in enumerate(units):
                load(rounds(MIX0), c, src)
                if c == SLOTS:
                    sp.wait_ge(unit_done, MIX0)
                    sp.dma_start(decay_sb[:], decay).then_inc(mix_landed, 16)
                    sp.dma_start(pool_w_sb[:], pool_w).then_inc(mix_landed, 16)
                    sp.dma_start(edge_sb[:], edge).then_inc(mix_landed, 16)
            with sp.Fori(0, KF // 2) as i:
                load_gate_up(1, i)
            with sp.Fori(0, 2) as i:
                load_down(1, i)

            for n in range(Y_DVE):
                sp.wait_ge(y_dve, n + 1)
                sp.dma_start(outT[:, n, :], x[:, n, :]).then_inc(stored, 16)
                if Y_DVE + n < KD:
                    sp.wait_ge(y_pool, n + 1)
                    sp.dma_start(outT[:, Y_DVE + n, :], x[:, Y_DVE + n, :]).then_inc(stored, 16)
            sp.wait_ge(stored, 16 * KD)

        @block.tensor
        def _(pe):
            def product(out, pairs, first, last):
                for r, (lhs, rhs) in enumerate(pairs):
                    mm = nc.tensor.matmul(out, lhs, rhs, start=first and r == 0,
                                          stop=last and r == 2)
                return mm

            def weights_still(out, s, c, hi, lo, first, last):
                wh, wl = (w[:, s, c * P:(c + 1) * P] for w in (w_hi, w_lo))
                return product(out, ((wh, hi), (wh, lo), (wl, hi)), first, last)

            def weights_moving(out, s, c, hi, lo, first, last):
                wh, wl = (w[:, s, c * T:(c + 1) * T] for w in (w_hi, w_lo))
                return product(out, ((hi, wh), (lo, wh), (hi, wl)), first, last)

            def column_tile(n, s, bank, norm=None):
                pe.wait_ge(lo_split, n + 1)
                for k in range(KD):
                    if norm is not None:
                        pe.wait_ge(h_ready, KD * norm + k + 1)
                    mm = weights_still(ps[:, bank, :], s, k, h_hi[:, k, :], h_lo[:, k, :],
                                       k == 0, k == KD - 1)
                mm.then_inc(unit_done, 1)

            def token_tiles(n0, bank0):
                for c in range(SLOTS):
                    pe.wait_ge(lo_split, n0 + c + 1)
                    for kk in range(2):
                        k = 2 * c + kk
                        for t in range(TT):
                            mm = weights_moving(ps[:, bank0 + t, :], c, kk,
                                                h_hi[:, k, t * P:(t + 1) * P],
                                                h_lo[:, k, t * P:(t + 1) * P],
                                                k == 0, k == KD - 1)
                    mm.then_inc(unit_done, 1)
                    yield c

            def mean_square(norm):
                pe.wait_ge(ssq_added, KD * (norm + 1))
                nc.tensor.matmul(ps[:, NORM_BANK, :], mean_w[:], ssq[:, 0, :],
                                 start=True, stop=True).then_inc(mean_done, 1)

            def gate_up(f, i, norm=None):
                for m in range(2):
                    ft = KF * f + 2 * i + m
                    n = GU0[f] + 4 * i + 2 * m
                    if known(ft, 2):
                        pe.wait_ge(gate_scaled, ft - 1)
                    column_tile(n, 2 * m, 2 * m, norm if m == 0 else None)
                    if known(ft, 2):
                        pe.wait_ge(up_scaled, ft - 1)
                    column_tile(n + 1, 2 * m + 1, 2 * m + 1)
                    if m == 0 and norm is not None:
                        mean_square(norm)

            def down_tiles(f, i):
                for j in range(4):
                    for r, (k0, k1) in enumerate(DOWN_PARTS):
                        c = 3 * j + r
                        pe.wait_ge(lo_split, DOWN0[f] + 12 * i + c + 1)
                        pe.wait_ge(a_lo_ready, KF * f + k1)
                        for k in range(k0, k1):
                            mm = weights_still(at(ps, 4 - 4 * i + j), c % SLOTS, k - k0,
                                               a_hi[:, k, :], a_lo[:, k, :], k == 0, k == KF - 1)
                        mm.then_inc(unit_done, 1)

            def scores(h):
                rows = slice(DK * (h % 2), DK * (h % 2) + DK)
                for j, (bank, col) in enumerate(SCORE_AT):
                    mm = nc.tensor.matmul(ps[:, bank, col:col + T - P * j],
                                          qk[rows, 2 + h // 2, P * j:P * (j + 1)],
                                          qk[rows, h // 2, P * j:T], start=True, stop=True)
                mm.then_inc(scores_done, 1)

            def attend(h):
                for i in range(TT):
                    for j in range(i + 1):
                        at_i = PT_AT[j] + P * (i - j)
                        mm = nc.tensor.matmul(ps[:, h, P * i:P * (i + 1)],
                                              pt[:, h, at_i:at_i + P],
                                              v[:, j, DV * h:DV * (h + 1)],
                                              start=j == 0, stop=j == i)
                mm.then_inc(pv_done, 1)

            def pooled_product(s):
                pe.wait_ge(pooled_ready, s + 1)
                nc.tensor.matmul(ps[:, U_BANK[s], :], pool_w_sb[:, 3 - s, :],
                                 u_sb[:, s % 2, :], start=True, stop=True).then_inc(cat_done, 1)

            def turn(h):
                pe.wait_ge(ret_ready, h + 1)
                for t in range(TT):
                    mm = nc.tensor.transpose(ps[:, h, P * t:P * (t + 1)],
                                             n_sb[:, h % 2, P * t:P * (t + 1)], ident[:])
                mm.then_inc(cat_done, 1)

            def out_part(j, ks):
                for k in ks:
                    if j < 2:
                        pe.wait_ge(cat_ready, cat_count(k))
                    mm = weights_still(ps[:, U_BANK[j % 4], :], j % SLOTS, k, cat_hi[:, k, :],
                                       cat_lo[:, k, :], k == CAT_FIRST[0], k == CAT_LAST[0])
                    if k == CAT_LAST[0]:
                        mm.then_inc(unit_done, 1)

            pe.wait_ge(setup_done, 1)
            gate_up(0, 0, NORM_FFN[0])
            with pe.Fori(1, KF // 2) as i:
                gate_up(0, i)
            with pe.Fori(0, 2) as i:
                down_tiles(0, i)

            pe.wait_ge(x_updated, 5)
            for m in range(4):
                if m:
                    pe.wait_ge(x_updated, 5 + m)
                column_tile(MIX0 + QK0 + m, m, m, NORM_MIX if m == 0 else None)
                if m == 0:
                    mean_square(NORM_MIX)
                    for t in range(TT):
                        mm = nc.tensor.matmul(ps[:, TOK_BANK, t:t + 1],
                                              ssq[:, 0, P * t:P * (t + 1)], mean_w[:, 0:1],
                                              start=True, stop=True)
                    mm.then_inc(tok_mean_done, 1)
            pe.wait_ge(rms_ready, NORM_MIX + 1)
            pe.wait_ge(tok_rms_ready, 1)
            for c in token_tiles(MIX0 + V0, 4):
                pass
            pe.wait_ge(rot_ready, 4)
            for h in token_tiles(MIX0 + G0, 0):
                if h == 0:
                    pe.wait_ge(v_ready, TT)
                    pe.wait_ge(qk_ready, 4)
                else:
                    pe.wait_ge(pt_ready, h)
                scores(h)
            for s in range(4):
                if s == 1:
                    pe.wait_ge(pt_ready, HEADS)
                column_tile(MIX0 + U0 + s, s, U_BANK[s])
                if s == 0:
                    pe.wait_ge(sg_ready, TT)
                    pe.wait_ge(pt_ready, HEADS)
                attend(s)
                for event in CAT_AFTER[s]:
                    (pooled_product if event[0] == "y" else turn)(int(event[1]))
            for j in range(2):
                pe.wait_ge(lo_split, MIX0 + O0 + j + 1)
            out_part(0, CAT_FIRST)
            turn(2)
            out_part(1, CAT_FIRST)
            pooled_product(3)
            turn(3)
            for ks in (CAT_NEXT, CAT_LAST):
                for j in range(2):
                    out_part(j, ks)
            for j in range(2, KD):
                pe.wait_ge(lo_split, MIX0 + O0 + j + 1)
                if j >= 4:
                    pe.wait_ge(x_updated, KD + j - 3)
                out_part(j, CAT_FIRST + CAT_NEXT + CAT_LAST)

            gate_up(1, 0, NORM_FFN[1])
            with pe.Fori(1, KF // 2) as i:
                gate_up(1, i)
            with pe.Fori(0, 2) as i:
                down_tiles(1, i)
            mean_square(NORM_OUT)

        @block.scalar
        def _(act):
            def split(rnd, c):
                n, s = SLOTS * rnd + c, c % SLOTS
                act.wait_ge(raw_landed[s], 16 * (rnd + c // SLOTS + 1))
                if known(n, SLOTS):
                    act.wait_ge(unit_done, n - SLOTS + 1)
                nc.scalar.activation(w_hi[:, s, :], w_raw[:, s, :], ACT.Copy).then_inc(hi_split, 1)

            def hi_of_h(norm, j, ready):
                ready()
                nc.scalar.activation(at(h_hi, j), at(x, j), ACT.Copy,
                                     scale=gain[:, bass.ds(GAIN_NORM[norm] + j, 1)]
                                     ).then_inc(h_hi_ready, 1)

            def square_of(norm, j, b):
                c = KD * norm + j
                if known(c, 2):
                    act.wait_ge(ssq_added, c - 1)
                nc.scalar.activation(at(square, b), at(x, j), ACT.Square
                                     ).then_inc(square_ready, 1)

            def next_norm(norm, j, b, last=False):
                def ready():
                    act.wait_ge(x_updated, KD * (norm - 1) + j + 1)
                if last:
                    ready()
                else:
                    hi_of_h(norm, j, ready)
                square_of(norm, j, b)

            def take_rms(norm):
                act.wait_ge(mean_done, norm + 1)
                nc.scalar.activation(rms[:, 0, :], ps[:, NORM_BANK, :], ACT.Sqrt,
                                     bias=eps[:, 0:1]).then_inc(rms_ready, 1)

            def activate(f, i, m):
                ft = KF * f + 2 * i + m
                act.wait_ge(gate_scaled, ft + 1)
                nc.scalar.activation(tmp_a[:, 0, :], tmp_a[:, 0, :], ACT.Silu
                                     ).then_inc(silu_ready, 1)

            def gate_up(f, i, norm=None):
                for m in range(2):
                    split(rounds(GU0[f]) + i, 2 * m + AHEAD)
                    split(rounds(GU0[f]) + i, 2 * m + AHEAD + 1)
                    if m == 0 and norm is not None:
                        take_rms(norm)
                    activate(f, i, m)

            def down_tiles(f, i, upto=12 + AHEAD):
                for j in range(4):
                    for c in range(3 * j + AHEAD, min(3 * j + 3 + AHEAD, upto)):
                        split(rounds(DOWN0[f]) + 3 * i, c)
                    next_norm((NORM_MIX, NORM_OUT)[f], 4 * i + j, j % 2, last=f == 1)

            def hi_of_cat(event):
                bank, k, g = cat_place(event)
                act.wait_ge(cat_done, CAT_EVENTS.index(event) + 1)
                nc.scalar.activation(cat_hi[:, k, :], ps[:, bank, :], ACT.Copy,
                                     scale=gain[:, g:g + 1]).then_inc(cat_hi_ready, 1)

            def group_std(h):
                act.wait_ge(var_ready, h + 1)
                nc.scalar.activation(gn_std[:], meanvar[:, :, 1], ACT.Sqrt,
                                     bias=eps[:, 1:2]).then_inc(gn_std_ready, 1)

            act.dma_start(gain[:], gains).then_inc(gain_landed, 16)
            for k in range(KD):
                act.dma_start(x[:, k, :], xT[:, k, :]).then_inc(x_landed[k], 16)
            act.dma_start(rope_sb[:], rope).then_inc(rope_landed, 16)
            act.wait_ge(setup_done, 1)

            split(0, 0)
            act.wait_ge(gain_landed, 16)
            for j in range(KD):
                hi_of_h(NORM_FFN[0], j, lambda: act.wait_ge(x_landed[j], 16))
                if j == 3:
                    split(0, 1)
            for j in range(KD):
                square_of(NORM_FFN[0], j, j % 2)
            gate_up(0, 0, NORM_FFN[0])
            with act.Fori(1, KF // 2) as i:
                gate_up(0, i)
            for i in range(2):
                down_tiles(0, i)

            for n in range(MIX_UNITS):
                split(rounds(MIX0), n + AHEAD)
                if n == QK0:
                    take_rms(NORM_MIX)
                    act.wait_ge(tok_mean_done, 1)
                    nc.scalar.activation(rms_tok[:], ps[:, TOK_BANK, 0:TT], ACT.Sqrt,
                                         bias=eps[:, 0:1]).then_inc(tok_rms_ready, 1)
                if n == V0 + 3:
                    act.wait_ge(tok_rstd_ready, 1)
                    act.wait_ge(unit_done, MIX0 + n + 1)
                    for t in range(TT):
                        nc.scalar.activation(v[:, t, :], ps[:, 4 + t, :], ACT.Copy,
                                             scale=rstd_tok[:, t:t + 1]).then_inc(v_ready, 1)
                if n == G0 + 3:
                    act.wait_ge(unit_done, MIX0 + n + 1)
                    for t in range(TT):
                        nc.scalar.activation(sg[:, t, :], ps[:, t, :], ACT.Silu,
                                             scale=rstd_tok[:, t:t + 1]).then_inc(sg_ready, 1)
                if U0 <= n < O0:
                    for task, arg in RET_TASKS[n - U0]:
                        if task == "cat":
                            hi_of_cat(arg)
                        if task == "stats":
                            group_std(arg)
                if n >= O0:
                    next_norm(NORM_FFN[1], n - O0, n % 2)

            gate_up(1, 0, NORM_FFN[1])
            with act.Fori(1, KF // 2) as i:
                gate_up(1, i)
            down_tiles(1, 0)
            down_tiles(1, 1, upto=12)
            for j in range(Y_DVE, KD):
                nc.scalar.activation(x[:, j, :], x[:, j, :], ACT.Copy,
                                     scale=gain[:, GAIN_NORM[NORM_OUT] + j:
                                                GAIN_NORM[NORM_OUT] + j + 1]
                                     ).then_inc(final_gained, 1)
            take_rms(NORM_OUT)

        @block.vector
        def _(dve):
            def split(rnd, c):
                n, s = SLOTS * rnd + c, c % SLOTS
                dve.wait_ge(hi_split, n + 1)
                nc.vector.tensor_tensor(w_lo[:, s, :], w_raw[:, s, :],
                                        w_hi[:, s, :].bitcast(F32), ALU.subtract
                                        ).then_inc(lo_split, 1)

            def lo_of_h(norm, j):
                dve.wait_ge(h_hi_ready, KD * norm + j + 1)
                nc.vector.scalar_tensor_tensor(
                    out=at(h_lo, j), in0=at(x, j),
                    scalar=gain[:, bass.ds(GAIN_NORM[norm] + j, 1)],
                    in1=at(h_hi, j).bitcast(F32), op0=ALU.mult, op1=ALU.subtract
                    ).then_inc(h_ready, 1)

            def update_x(norm, j, bank, n, factor, last=False):
                dve.wait_ge(unit_done, n + 1)
                nc.vector.scalar_tensor_tensor(out=at(x, j), in0=at(ps, bank), scalar=factor,
                                               in1=at(x, j), op0=ALU.mult, op1=ALU.add
                                               ).then_inc(x_updated, 1)
                if not last:
                    lo_of_h(norm, j)

            def take_rstd(norm):
                dve.wait_ge(rms_ready, norm + 1)
                nc.vector.reciprocal(rstd[:, 0, :], rms[:, 0, :]).then_inc(rstd_ready, 1)

            def activate(f, i, m):
                ft = KF * f + 2 * i + m
                n = GU0[f] + 4 * i + 2 * m
                dve.wait_ge(unit_done, n + 1)
                nc.vector.tensor_tensor(tmp_a[:, 0, :], ps[:, 2 * m, :], rstd[:, 0, :], ALU.mult
                                        ).then_inc(gate_scaled, 1)
                dve.wait_ge(unit_done, n + 2)
                if known(ft, 1):
                    dve.wait_ge(a_lo_ready, ft)
                nc.vector.tensor_tensor(tmp_b[:, 0, :], ps[:, 2 * m + 1, :], rstd[:, 0, :],
                                        ALU.mult).then_inc(up_scaled, 1)
                dve.wait_ge(up_scaled, ft + 1)
                dve.wait_ge(silu_ready, ft + 1)
                nc.vector.tensor_tensor(at(a_hi, 2 * i + m), tmp_a[:], tmp_b[:], ALU.mult)
                nc.vector.tensor_tensor(tmp_b[:], tmp_a[:], tmp_b[:], ALU.mult).then_inc(a_ready, 1)
                dve.wait_ge(a_ready, ft + 1)
                nc.vector.tensor_tensor(at(a_lo, 2 * i + m), at(tmp_b, 0),
                                        at(a_hi, 2 * i + m).bitcast(F32), ALU.subtract
                                        ).then_inc(a_lo_ready, 1)

            def gate_up(f, i, norm=None):
                for m in range(2):
                    split(rounds(GU0[f]) + i, 2 * m + AHEAD)
                    split(rounds(GU0[f]) + i, 2 * m + AHEAD + 1)
                    if m == 0 and norm is not None:
                        take_rstd(norm)
                        dve.wait_ge(rstd_ready, norm + 1)
                    activate(f, i, m)

            def down_tiles(f, i, upto=12 + AHEAD):
                for j in range(4):
                    for c in range(3 * j + AHEAD, min(3 * j + 3 + AHEAD, upto)):
                        split(rounds(DOWN0[f]) + 3 * i, c)
                    update_x((NORM_MIX, NORM_OUT)[f], 4 * i + j, 4 - 4 * i + j,
                             DOWN0[f] + 12 * i + 3 * j + 2, 0.5, last=f == 1)

            def rotate(m):
                dve.wait_ge(unit_done, MIX0 + QK0 + m + 1)
                if m:
                    dve.wait_ge(qk_ready, m)
                nc.vector.tensor_tensor(rot_a[:, 0, :], ps[:, m, :], tmp_a[:, 0, :], ALU.mult)
                for src in range(0, P, DK // 2):
                    dst = src ^ (DK // 2)
                    last = nc.vector.tensor_tensor(rot_b[dst:dst + DK // 2, 0, :],
                                                   ps[src:src + DK // 2, m, :],
                                                   tmp_b[src:src + DK // 2, 0, :], ALU.mult)
                last.then_inc(rot_ready, 1)

            def decay_scores(h):
                dve.wait_ge(scores_done, h + 1)
                for j, (bank, col) in enumerate(SCORE_AT):
                    w = T - P * j
                    last = nc.vector.tensor_tensor(pt[:, h, PT_AT[j]:PT_AT[j] + w],
                                                   ps[:, bank, col:col + w],
                                                   decay_sb[:, h, 0:w], ALU.mult)
                last.then_inc(pt_ready, 1)

            def take_u(s):
                dve.wait_ge(unit_done, MIX0 + U0 + s + 1)
                if s >= 2:
                    dve.wait_ge(cat_done, CAT_EVENTS.index(f"y{s - 2}") + 1)
                nc.vector.tensor_tensor(u_sb[:, s % 2, :], ps[:, U_BANK[s], :], rstd[:, 0, :],
                                        ALU.mult).then_inc(u_ready, 1)

            def window_mean(s):
                w = WINDOWS[3 - s]
                levels = w.bit_length() - 1
                total = (rot_a, rot_b)[(levels - 1) % 2]
                dve.wait_ge(sum_ready, s + 1)
                nc.vector.tensor_tensor(total[:, 0, 0:16], total[:, 0, 0:16], edge_sb[:, 3 - s, :],
                                        ALU.mult).then_inc(edge_done, 1)
                dve.wait_ge(edge_done, s + 1)
                nc.vector.scalar_tensor_tensor(out=u_sb[:, s % 2, :], in0=total[:, 0, :],
                                               scalar=1.0 / w, in1=u_sb[:, s % 2, :],
                                               op0=ALU.mult, op1=ALU.subtract
                                               ).then_inc(pooled_ready, 1)

            def group_stats(h):
                dve.wait_ge(pv_done, h + 1)
                for t in range(TT):
                    last = nc.vector.bn_stats(stats[:, t, :], ps[:, h, P * t:P * (t + 1)])
                last.then_inc(stats_ready, 1)
                dve.wait_ge(stats_ready, h + 1)
                for t in range(TT):
                    last = nc.vector.bn_aggr(meanvar[:, t, :], stats[:, t, :])
                last.then_inc(var_ready, 1)

            def group_norm(h):
                dve.wait_ge(gn_std_ready, h + 1)
                nc.vector.reciprocal(gn_rstd[:], gn_std[:]).then_inc(gn_rstd_ready, 1)
                dve.wait_ge(gn_rstd_ready, h + 1)
                if h >= 2:
                    dve.wait_ge(cat_done, CAT_EVENTS.index(f"t{h - 2}") + 1)
                for t in range(TT):
                    last = nc.vector.tensor_scalar(n_sb[:, h % 2, P * t:P * (t + 1)],
                                                   ps[:, h, P * t:P * (t + 1)],
                                                   meanvar[:, t, 0:1], gn_rstd[:, t:t + 1],
                                                   ALU.subtract, ALU.mult)
                last.then_inc(gn_scaled, 1)
                dve.wait_ge(gn_scaled, h + 1)
                n3 = n_sb[:, h % 2, :].rearrange("p (t c) -> p t c", t=TT)
                nc.vector.tensor_tensor(n3, n3, sg[:, :, DV * h:DV * (h + 1)], ALU.mult
                                        ).then_inc(ret_ready, 1)

            def lo_of_cat(event):
                bank, k, g = cat_place(event)
                dve.wait_ge(cat_hi_ready, CAT_EVENTS.index(event) + 1)
                nc.vector.scalar_tensor_tensor(out=cat_lo[:, k, :], in0=ps[:, bank, :],
                                               scalar=gain[:, g:g + 1],
                                               in1=cat_hi[:, k, :].bitcast(F32),
                                               op0=ALU.mult, op1=ALU.subtract
                                               ).then_inc(cat_ready, 1)

            split(0, 0)
            dve.wait_ge(gain_landed, 16)
            for j in range(KD):
                dve.wait_ge(x_landed[j], 16)
                lo_of_h(NORM_FFN[0], j)
                if j == 3:
                    split(0, 1)
            gate_up(0, 0, NORM_FFN[0])
            with dve.Fori(1, KF // 2) as i:
                gate_up(0, i)
            with dve.Fori(0, 2) as i:
                down_tiles(0, i)

            for n in range(MIX_UNITS):
                split(rounds(MIX0), n + AHEAD)
                if n == QK0:
                    take_rstd(NORM_MIX)
                    dve.wait_ge(tok_rms_ready, 1)
                    nc.vector.reciprocal(rstd_tok[:], rms_tok[:]).then_inc(tok_rstd_ready, 1)
                    dve.wait_ge(rstd_ready, NORM_MIX + 1)
                    dve.wait_ge(rope_landed, 16)
                    for r, t in enumerate((tmp_a, tmp_b)):
                        nc.vector.tensor_tensor(t[:, 0, :], rope_sb[:, r, :], rstd[:, 0, :],
                                                ALU.mult).then_inc(rope_scaled, 1)
                    dve.wait_ge(rope_scaled, 2)
                if n < V0:
                    rotate(n)
                if G0 <= n < U0:
                    if n == G0:
                        dve.wait_ge(mix_landed, 48)
                    decay_scores(n - G0)
                if U0 <= n < O0:
                    for task, arg in RET_TASKS[n - U0]:
                        {"u": take_u, "mean": window_mean, "stats": group_stats,
                         "norm": group_norm, "cat": lo_of_cat}[task](arg)
                if n >= O0:
                    update_x(NORM_FFN[1], n - O0, U_BANK[(n - O0) % 4], MIX0 + n, 1.0)

            gate_up(1, 0, NORM_FFN[1])
            with dve.Fori(1, KF // 2) as i:
                gate_up(1, i)
            down_tiles(1, 0)
            down_tiles(1, 1, upto=12)
            take_rstd(NORM_OUT)
            dve.wait_ge(rstd_ready, NORM_OUT + 1)
            for j in range(Y_DVE):
                g = GAIN_NORM[NORM_OUT] + j
                nc.vector.scalar_tensor_tensor(out=x[:, j, :], in0=x[:, j, :],
                                               scalar=gain[:, g:g + 1], in1=rstd[:, 0, :],
                                               op0=ALU.mult, op1=ALU.mult).then_inc(y_dve, 1)

        @block.gpsimd
        def _(pool):
            def sum_squares(norm, j, b):
                c = KD * norm + j
                pool.wait_ge(square_ready, c + 1)
                if known(c, 1):
                    pool.wait_ge(ssq_added, c)
                nc.gpsimd.tensor_tensor(ssq[:, 0, :], ssq[:, 0, :], square[:, b, :], ALU.add
                                        ).then_inc(ssq_added, 1)

            def clear_squares(norm):
                if norm:
                    pool.wait_ge(mean_done, norm)
                if norm == NORM_MIX + 1:
                    pool.wait_ge(tok_mean_done, 1)
                nc.gpsimd.memset(ssq[:], 0.0).then_inc(ssq_cleared, 1)
                pool.wait_ge(ssq_cleared, norm + 1)

            def window_sums(s):
                pool.wait_ge(u_ready, s + 1)
                if s:
                    pool.wait_ge(pooled_ready, s)
                src, d, l = u_sb[:, s % 2, :], 1, 0
                while d < WINDOWS[3 - s]:
                    dst = (rot_a, rot_b)[l % 2][:, 0, :]
                    nc.gpsimd.tensor_copy(dst[:, 0:d], src[:, 0:d])
                    add = nc.gpsimd.tensor_tensor(dst[:, d:T], src[:, d:T], src[:, 0:T - d],
                                                  ALU.add)
                    src, d, l = dst, 2 * d, l + 1
                    if d < WINDOWS[3 - s]:
                        add.then_inc(sum_step, 1)
                        pool.wait_ge(sum_step, SUM_STEPS[s] + l)
                add.then_inc(sum_ready, 1)

            nc.gpsimd.memset(mean_w[:], 1.0 / D)
            nc.gpsimd.memset(eps[:, 0:1], RMS_EPS)
            nc.gpsimd.memset(eps[:, 1:2], GN_EPS)
            nc.gpsimd.memset(ident[:], 0.0).then_inc(setup_step, 1)
            pool.wait_ge(setup_step, 1)
            nc.gpsimd.affine_select(out=ident[:], in_=ident[:], compare_op=ALU.not_equal, fill=1.0,
                                    base=0, pattern=[[-1, P]], channel_multiplier=1
                                    ).then_inc(setup_done, 1)

            clear_squares(0)
            for j in range(KD):
                sum_squares(0, j, j % 2)
            clear_squares(NORM_MIX)
            with pool.Fori(0, KD // 2) as i:
                for b in range(2):
                    sum_squares(NORM_MIX, 2 * i + b, b)
            for m in range(4):
                pool.wait_ge(rot_ready, m + 1)
                nc.gpsimd.tensor_tensor(qk[:, m, :], rot_a[:, 0, :], rot_b[:, 0, :], ALU.add
                                        ).then_inc(qk_ready, 1)
            for s in range(4):
                window_sums(s)
            for norm in (NORM_FFN[1], NORM_OUT):
                clear_squares(norm)
                with pool.Fori(0, KD // 2) as i:
                    for b in range(2):
                        sum_squares(norm, 2 * i + b, b)
            pool.wait_ge(rstd_ready, NORM_OUT + 1)
            for j in range(Y_DVE, KD):
                pool.wait_ge(final_gained, j - Y_DVE + 1)
                nc.gpsimd.tensor_tensor(x[:, j, :], x[:, j, :], rstd[:, 0, :], ALU.mult
                                        ).then_inc(y_pool, 1)


def decay_table():
    gamma = 1.0 - 2.0 ** (-5.0 - np.arange(HEADS))
    key, query = np.arange(P)[:, None], np.arange(T)[None, :]
    seen = query // CHUNK >= key // CHUNK
    dist = np.abs(query - key)
    return np.stack([np.where(seen, g ** dist, 0.0) * DK ** -0.5 for g in gamma],
                    axis=1).astype(np.float32)


def rope_table():
    half = DK // 2
    f = np.arange(P) % half
    freq = (ROPE_BASE ** (-f * 2.0 / DK)).astype(np.float32)
    ang = (np.arange(T, dtype=np.float32)[None, :] * freq[:, None]).astype(np.float64)
    sign = np.where(np.arange(P) % DK < half, 1.0, -1.0)[:, None]
    return np.stack([np.cos(ang), sign * np.sin(ang)], axis=1).astype(np.float32)


def edge_table():
    t = np.arange(16) + 1
    rows = np.stack([w / np.minimum(t, w) for w in WINDOWS])
    return np.broadcast_to(rows, (P,) + rows.shape).astype(np.float32).copy()


def kernel(**inputs):
    import concourse.bacc as bacc
    from concourse.bass_utils import run_bass_kernel_spmd

    w = {k: np.asarray(a) for k, a in inputs.items()}

    def columns(a):
        k, m = a.shape
        return np.ascontiguousarray(a.reshape(k // P, P, m // P, P).transpose(2, 1, 0, 3)
                                    .reshape(m // P, P, k))

    def k_pairs(a):
        return a.reshape(4, 2, P, T).transpose(0, 2, 1, 3).reshape(4, P, 2 * T)

    def by_feature(a):
        return a.reshape(-1, P).T

    w_in = w["w_in"][0]
    qk_cols, v_end, g_end = 2 * HEADS * DK, 2 * HEADS * DK + HEADS * DV, 2 * HEADS * (DK + DV)
    arrays = {
        "xT": np.ascontiguousarray(w["x"][0].T.reshape(KD, P, T).transpose(1, 0, 2)),
        "gate": columns(w["ffn1_gate"][0]), "up": columns(w["ffn1_up"][0]),
        "down": columns(w["ffn1_down"][0]),
        "gate2": columns(w["ffn2_gate"][0]), "up2": columns(w["ffn2_up"][0]),
        "down2": columns(w["ffn2_down"][0]),
        "w_qku": np.concatenate([columns(w_in[:, :qk_cols]), columns(w_in[:, g_end:])]),
        "w_vg": np.concatenate([k_pairs(w_in[:, qk_cols:v_end]), k_pairs(w_in[:, v_end:g_end])]),
        "w_out": columns(w["w_out"][0]),
        "pool_w": np.ascontiguousarray(w["pool_w"][0].transpose(1, 0, 2)),
        "gains": np.ascontiguousarray(np.concatenate(
            [by_feature(a) for a in (w["norm_ffn1"], w["norm_mix"], w["norm_ffn2"],
                                     w["norm_final"], w["ret_gn_gain"], w["pool_scale"])], axis=1)),
        "decay": decay_table(), "rope": rope_table(), "edge": edge_table(),
    }
    nc = bacc.Bacc("TRN2", target_bir_lowering=False, num_devices=1)
    args = [nc.dram_tensor(f"{n}_dram", a.shape, mybir.dt.from_np(a.dtype),
                           kind="ExternalInput").ap() for n, a in arrays.items()]
    args.append(nc.dram_tensor("outT_dram", (P, KD, T), F32, kind="ExternalOutput").ap())
    program(nc, *args)
    r = run_bass_kernel_spmd(nc, [{f"{n}_dram": a for n, a in arrays.items()}], core_ids=[0])
    out = r.results[0]["outT_dram"]
    return np.ascontiguousarray(out.transpose(1, 0, 2).reshape(D, T).T)[None]
```

```python
from contextlib import ExitStack

import numpy as np

import concourse.bass as bass
from concourse import mybir

F32 = mybir.dt.float32
F32R = mybir.dt.float32r
ACT = mybir.ActivationFunctionType
ALU = mybir.AluOpType

P = 128
D = 1024
T = 512
FF = 2816
KD = D // P
KF = FF // P
TT = T // P
HEADS = 4
DK = 64
DV = 128
CHUNK = 64
WINDOWS = (2, 4, 8, 16)
RMS_EPS = 1e-6
GN_EPS = 1e-5
ROPE_BASE = 10000.0

SLOTS = 4
UNIT = 1024
AHEAD = 2
DOWN_PARTS = ((0, 8), (8, 15), (15, 22))
LAST_UNITS = KF // 2
LAST_JOINT = 3

GU_UNITS = 2 * KF
DOWN_UNITS = len(DOWN_PARTS) * KD
MIX_UNITS = 24
GU0 = (0, GU_UNITS + DOWN_UNITS + MIX_UNITS)
DOWN0 = (GU0[0] + GU_UNITS, GU0[1] + GU_UNITS)
MIX0 = DOWN0[0] + DOWN_UNITS
QK0, V0, G0, U0, O0 = 0, 4, 8, 12, 16

GAIN_NORM = (0, 8, 16)
GAIN_RET = 24
GAIN_POOL = 28
GAINS = 32

NORM_FFN = (0, 2)
NORM_MIX = 1

SCORE_AT = ((4, 0), (5, 0), (6, 0), (5, 384))
PT_AT = (0, 512, 896, 1152)
PT = 1280
CAT_FIRST, CAT_NEXT, CAT_LAST = (7, 6, 5, 0, 1), (4, 2), (3,)
U_BANK = (7, 4, 5, 6)


NORM_BANK, TOK_BANK = 4, 5

CAT_EVENTS = ("y0", "y1", "t0", "y2", "t1", "t2", "y3", "t3")
CAT_AFTER = ((), ("y0",), ("y1", "t0"), ("y2", "t1"))
RET_TASKS = (
    (("u", 0), ("stats", 0), ("norm", 0), ("mean", 0)),
    (("u", 1), ("stats", 1), ("norm", 1), ("mean", 1), ("cat", "y0")),
    (("u", 2), ("stats", 2), ("cat", "y1"), ("cat", "t0"), ("norm", 2), ("mean", 2)),
    (("u", 3), ("mean", 3), ("cat", "y2"), ("cat", "t1"), ("stats", 3), ("norm", 3),
     ("cat", "t2"), ("cat", "y3"), ("cat", "t3")),
)
SUM_STEPS = (0, 3, 5, 6)


def cat_place(event):
    n = int(event[1])
    if event[0] == "y":
        return U_BANK[n], HEADS + 3 - n, GAIN_POOL + 3 - n
    return n, n, GAIN_RET + n


def added(norm, j):
    return 4 + KD * (norm - 1) + j + 1 if norm else 4


def cat_count(k):
    return 1 + [cat_place(e)[1] for e in CAT_EVENTS].index(k)


def program(nc, xT, gate, up, down, gate2, up2, down2, w_qku, w_vg, w_out, pool_w, gains,
            last_gain, decay, rope, edge, out):
    with ExitStack() as ctx:
        def sb(name, shape, dt=F32, scope=ctx):
            return scope.enter_context(nc.sbuf_tensor(name, shape, dt))

        def sem(name):
            return ctx.enter_context(nc.semaphore(name))

        x = sb("x_sb", [P, KD, T])
        h_hi = sb("h_hi", [P, KD, T], F32R)
        h_lo = sb("h_lo", [P, KD, T], F32R)
        w_raw = sb("w_raw", [P, SLOTS, UNIT])
        w_hi = sb("w_hi", [P, SLOTS, UNIT], F32R)
        w_lo = sb("w_lo", [P, SLOTS, UNIT], F32R)
        rstd = sb("rstd", [P, 1, T])
        rms = sb("rms", [P, 1, T])
        ssq = sb("ssq", [P, 1, T])
        square = sb("square", [P, 2, T])
        tmp_a = sb("tmp_a", [P, 1, T])
        tmp_b = sb("tmp_b", [P, 1, T])
        gain = sb("gain", [P, GAINS])
        rope_sb = sb("rope_sb", [P, 2, T])
        mean_w = sb("mean_w", [P, P])
        eps = sb("eps", [P, 2])
        rms_tok = sb("rms_tok", [P, TT])
        rstd_tok = sb("rstd_tok", [P, TT])
        ident = sb("ident", [P, P])
        warm = sb("warm", [P, 1])
        last_sum = sb("last_sum", [P, 2, TT])
        last_bias = sb("last_bias", [P, TT])
        stats = sb("stats", [P, TT, 6])
        meanvar = sb("meanvar", [P, TT, 2])
        gn_std = sb("gn_std", [P, TT])
        gn_rstd = sb("gn_rstd", [P, TT])

        with ExitStack() as ffn_scope:
            a_hi = sb("a_hi", [P, KF, T], F32R, ffn_scope)
            a_lo = sb("a_lo", [P, KF, T], F32R, ffn_scope)
        with ExitStack() as mix_scope:
            qk = sb("qk", [P, 4, T], scope=mix_scope)
            v = sb("v", [P, TT, HEADS * DV], scope=mix_scope)
            pt = sb("pt", [P, HEADS, PT], scope=mix_scope)
            sg = sb("sg", [P, TT, HEADS * DV], scope=mix_scope)
            cat_hi = sb("cat_hi", [P, KD, T], F32R, mix_scope)
            cat_lo = sb("cat_lo", [P, KD, T], F32R, mix_scope)
            decay_sb = sb("decay_sb", [P, HEADS, T], scope=mix_scope)
            pool_w_sb = sb("pool_w_sb", [P, HEADS, P], scope=mix_scope)
            edge_sb = sb("edge_sb", [P, len(WINDOWS), 16], scope=mix_scope)
            rot_a = sb("rot_a", [P, 1, T], scope=mix_scope)
            rot_b = sb("rot_b", [P, 1, T], scope=mix_scope)
        u_sb = qk[:, 0:2, :]
        n_sb = qk[:, 2:4, :]

        ps = ctx.enter_context(nc.psum_tensor("ps", [P, 8, T], F32))

        raw_landed = [sem(f"raw_landed{s}") for s in range(SLOTS)]
        hi_split = sem("hi_split")
        lo_split = sem("lo_split")
        unit_done = sem("unit_done")
        x_landed = [sem(f"x_landed{k}") for k in range(KD // 2)]
        half_landed = sem("half_landed")
        half_hi_split = sem("half_hi_split")
        half_split = sem("half_split")
        gain_landed = sem("gain_landed")
        rope_landed = sem("rope_landed")
        mix_landed = sem("mix_landed")
        setup_step = sem("setup_step")
        setup_done = sem("setup_done")
        x_updated = sem("x_updated")
        h_hi_ready = sem("h_hi_ready")
        h_ready = sem("h_ready")
        square_ready = sem("square_ready")
        ssq_cleared = sem("ssq_cleared")
        ssq_added = sem("ssq_added")
        odd_added = sem("odd_added")
        mean_done = sem("mean_done")
        rms_ready = sem("rms_ready")
        rstd_ready = sem("rstd_ready")
        tok_mean_done = sem("tok_mean_done")
        tok_rms_ready = sem("tok_rms_ready")
        tok_rstd_ready = sem("tok_rstd_ready")
        gate_scaled = sem("gate_scaled")
        up_scaled = sem("up_scaled")
        silu_ready = sem("silu_ready")
        a_ready = sem("a_ready")
        a_lo_ready = sem("a_lo_ready")
        rope_scaled = sem("rope_scaled")
        rot_ready = sem("rot_ready")
        qk_ready = sem("qk_ready")
        v_ready = sem("v_ready")
        sg_ready = sem("sg_ready")
        scores_done = sem("scores_done")
        pt_ready = sem("pt_ready")
        pv_done = sem("pv_done")
        u_ready = sem("u_ready")
        sum_step = sem("sum_step")
        sum_ready = sem("sum_ready")
        edge_done = sem("edge_done")
        pooled_ready = sem("pooled_ready")
        stats_ready = sem("stats_ready")
        var_ready = sem("var_ready")
        gn_std_ready = sem("gn_std_ready")
        gn_rstd_ready = sem("gn_rstd_ready")
        gn_scaled = sem("gn_scaled")
        ret_ready = sem("ret_ready")
        cat_done = sem("cat_done")
        cat_hi_ready = sem("cat_hi_ready")
        cat_ready = sem("cat_ready")
        last_gain_landed = sem("last_gain_landed")
        tile_done = sem("tile_done")
        last_square = sem("last_square")
        last_bias_ready = sem("last_bias_ready")
        last_gained = sem("last_gained")
        last_rms_ready = sem("last_rms_ready")
        last_rstd_ready = sem("last_rstd_ready")
        y_ready = sem("y_ready")
        stored = sem("stored")

        def at(t, i):
            return t[:, bass.ds(i, 1), :]

        def known(n, least):
            return not (isinstance(n, int) and n < least)

        def rounds(n0):
            return n0 // SLOTS

        def wait_last_tile(engine, dh, t):
            if t < TT - 1:
                engine.wait_ge(tile_done, (TT - 1) * dh + t + 1)
            else:
                engine.wait_ge(unit_done, DOWN0[1] + LAST_UNITS * (dh + 1))

        block = ctx.enter_context(nc.Block())

        @block.sync
        def _(sp):
            def load(rnd, c, src, width=UNIT):
                n, s = SLOTS * rnd + c, c % SLOTS
                if known(n, SLOTS):
                    sp.wait_ge(lo_split, n - SLOTS + 1)
                sp.dma_start(w_raw[:, s, 0:width], src).then_inc(raw_landed[s], 16)

            def load_gate_up(f, i):
                for c in range(4):
                    src = ((gate, up), (gate2, up2))[f][c % 2]
                    load(rounds(GU0[f]) + i, c,
                         src[bass.ds(2 * i + c // 2, 1), :, :].rearrange("a p c -> p (a c)"))

            def load_down(i):
                for j in range(4):
                    for r, (k0, k1) in enumerate(DOWN_PARTS):
                        load(rounds(DOWN0[0]) + 3 * i, 3 * j + r,
                             down[bass.ds(4 * i + j, 1), :, k0 * P:k1 * P]
                             .rearrange("a p c -> p (a c)"), (k1 - k0) * P)

            half = UNIT // 2
            sp.dma_start(w_raw[:, 0, 0:half], gate[0, :, 0:half]).then_inc(half_landed, 16)
            sp.dma_start(x[:, 0:2, :], xT[:, 0:2, :]).then_inc(x_landed[0], 16)
            sp.dma_start(w_raw[:, 0, half:UNIT], gate[0, :, half:UNIT]).then_inc(raw_landed[0], 16)
            for k in range(1, KD // 2):
                sp.dma_start(x[:, 2 * k:2 * k + 2, :], xT[:, 2 * k:2 * k + 2, :]
                             ).then_inc(x_landed[k], 16)
            for c in range(1, SLOTS):
                load(0, c, (gate, up)[c % 2][c // 2])
            with sp.Fori(1, KF // 2) as i:
                load_gate_up(0, i)
            with sp.Fori(0, 2) as i:
                load_down(i)
            units = ([w_qku[m] for m in range(4)] + [w_vg[m] for m in range(8)]
                     + [w_qku[7 - s] for s in range(4)] + [w_out[m] for m in range(KD)])
            for c, src in enumerate(units):
                load(rounds(MIX0), c, src)
                if c == SLOTS:
                    sp.wait_ge(unit_done, MIX0)
                    sp.dma_start(decay_sb[:], decay).then_inc(mix_landed, 16)
                    sp.dma_start(pool_w_sb[:], pool_w).then_inc(mix_landed, 16)
                    sp.dma_start(edge_sb[:], edge).then_inc(mix_landed, 16)
            with sp.Fori(0, KF // 2) as i:
                load_gate_up(1, i)
            sp.wait_ge(rope_scaled, 2)
            sp.dma_start(rope_sb[:].rearrange("p a t -> p (a t)"),
                         last_gain.partition_broadcast(P)).then_inc(last_gain_landed, 16)
            with sp.Fori(0, LAST_UNITS // 2) as i:
                for c in range(4):
                    load(rounds(DOWN0[1]) + i, c, down2[bass.ds(4 * i + c, 1), :, :]
                         .rearrange("a p c -> p (a c)"))
            for c in range(LAST_UNITS // 2 * 4, 2 * LAST_UNITS):
                load(rounds(DOWN0[1]), c, down2[c])

            rows = out.rearrange("(t p) (a c) -> p t a c", p=P, a=2)
            for t in range(TT - 1):
                sp.wait_ge(y_ready, 2 * t + 2)
                sp.dma_start(rows[:, t], x[:, t:KD:TT, :]).then_inc(stored, 16)
            for dh in range(2):
                sp.wait_ge(y_ready, 2 * TT - 1 + dh)
                sp.dma_start(rows[:, TT - 1, dh], x[:, TT * dh + TT - 1, :]).then_inc(stored, 16)
            sp.wait_ge(stored, 16 * (TT + 1))

        @block.tensor
        def _(pe):
            def product(out, pairs, first, last, onto=False):
                for r, (lhs, rhs) in enumerate(pairs):
                    mm = nc.tensor.matmul(out, lhs, rhs, start=first and r == 0,
                                          stop=last and r == 2, skip_group_check=onto)
                return mm

            def weights_still(out, s, c, hi, lo, first, last):
                wh, wl = (w[:, s, c * P:(c + 1) * P] for w in (w_hi, w_lo))
                return product(out, ((wh, hi), (wh, lo), (wl, hi)), first, last)

            def weights_moving(out, s, c, hi, lo, first, last, onto=False):
                wh, wl = (w[:, s, c * T:(c + 1) * T] for w in (w_hi, w_lo))
                return product(out, ((hi, wh), (lo, wh), (hi, wl)), first, last, onto)

            def column_tile(n, s, bank, norm=None):
                if known(n, 1):
                    pe.wait_ge(lo_split, n + 1)
                else:
                    pe.wait_ge(half_split, 1)
                for k in range(KD):
                    if k == KD // 2 and not known(n, 1):
                        pe.wait_ge(lo_split, 1)
                    if norm is not None:
                        pe.wait_ge(h_ready, KD * norm + k + 1)
                    mm = weights_still(ps[:, bank, :], s, k, h_hi[:, k, :], h_lo[:, k, :],
                                       k == 0, k == KD - 1)
                mm.then_inc(unit_done, 1)

            def token_tiles(n0, bank0):
                for c in range(SLOTS):
                    pe.wait_ge(lo_split, n0 + c + 1)
                    for kk in range(2):
                        k = 2 * c + kk
                        for t in range(TT):
                            mm = weights_moving(ps[:, bank0 + t, :], c, kk,
                                                h_hi[:, k, t * P:(t + 1) * P],
                                                h_lo[:, k, t * P:(t + 1) * P],
                                                k == 0, k == KD - 1)
                    mm.then_inc(unit_done, 1)
                    yield c

            def mean_square(norm):
                pe.wait_ge(ssq_added, added(norm, KD - 1))
                nc.tensor.matmul(ps[:, NORM_BANK, :], mean_w[:], ssq[:, 0, :],
                                 start=True, stop=True).then_inc(mean_done, 1)

            def gate_up(f, i, norm=None):
                for m in range(2):
                    ft = KF * f + 2 * i + m
                    n = GU0[f] + 4 * i + 2 * m
                    if known(ft, 2):
                        pe.wait_ge(gate_scaled, ft - 1)
                    column_tile(n, 2 * m, 2 * m, norm if m == 0 else None)
                    if known(ft, 2):
                        pe.wait_ge(up_scaled, ft - 1)
                    column_tile(n + 1, 2 * m + 1, 2 * m + 1)
                    if m == 0 and norm is not None:
                        mean_square(norm)

            def down_tiles(i):
                for j in range(4):
                    for r, (k0, k1) in enumerate(DOWN_PARTS):
                        c = 3 * j + r
                        pe.wait_ge(lo_split, DOWN0[0] + 12 * i + c + 1)
                        pe.wait_ge(a_lo_ready, k1)
                        for k in range(k0, k1):
                            mm = weights_still(at(ps, 4 - 4 * i + j), c % SLOTS, k - k0,
                                               a_hi[:, k, :], a_lo[:, k, :], k == 0, k == KF - 1)
                        mm.then_inc(unit_done, 1)

            def last_half(dh):
                def bank(t):
                    return ps[:, (TT if dh == 0 else 0) + t, :]

                def k_tile(t, c, kk):
                    k = 2 * c + kk
                    return weights_moving(bank(t), (LAST_UNITS * dh + c) % SLOTS, kk,
                                          a_hi[:, k, t * P:(t + 1) * P],
                                          a_lo[:, k, t * P:(t + 1) * P], False, k == KF - 1,
                                          onto=True)

                n0 = DOWN0[1] + LAST_UNITS * dh
                for t in range(TT):
                    for d in range(TT):
                        nc.tensor.matmul(bank(t)[:, P * d:P * (d + 1)],
                                         x[:, TT * dh + d, P * t:P * (t + 1)], ident[:],
                                         is_transpose=True, start=d == 0, stop=False,
                                         skip_group_check=True)
                for c in range(LAST_UNITS - LAST_JOINT):
                    pe.wait_ge(lo_split, n0 + c + 1)
                    pe.wait_ge(a_lo_ready, KF + 2 * c + 2)
                    for kk in range(2):
                        for t in range(TT):
                            mm = k_tile(t, c, kk)
                    mm.then_inc(unit_done, 1)
                pe.wait_ge(lo_split, n0 + LAST_UNITS)
                pe.wait_ge(a_lo_ready, 2 * KF)
                for t in range(TT):
                    for c in range(LAST_UNITS - LAST_JOINT, LAST_UNITS):
                        for kk in range(2):
                            mm = k_tile(t, c, kk)
                        if t == TT - 1:
                            mm.then_inc(unit_done, 1)
                    if t < TT - 1:
                        mm.then_inc(tile_done, 1)

            def scores(h):
                rows = slice(DK * (h % 2), DK * (h % 2) + DK)
                for j, (bank, col) in enumerate(SCORE_AT):
                    mm = nc.tensor.matmul(ps[:, bank, col:col + T - P * j],
                                          qk[rows, 2 + h // 2, P * j:P * (j + 1)],
                                          qk[rows, h // 2, P * j:T], start=True, stop=True)
                mm.then_inc(scores_done, 1)

            def attend(h):
                for i in range(TT):
                    for j in range(i + 1):
                        at_i = PT_AT[j] + P * (i - j)
                        mm = nc.tensor.matmul(ps[:, h, P * i:P * (i + 1)],
                                              pt[:, h, at_i:at_i + P],
                                              v[:, j, DV * h:DV * (h + 1)],
                                              start=j == 0, stop=j == i)
                mm.then_inc(pv_done, 1)

            def pooled_product(s):
                pe.wait_ge(pooled_ready, s + 1)
                nc.tensor.matmul(ps[:, U_BANK[s], :], pool_w_sb[:, 3 - s, :],
                                 u_sb[:, s % 2, :], start=True, stop=True).then_inc(cat_done, 1)

            def turn(h):
                pe.wait_ge(ret_ready, h + 1)
                for t in range(TT):
                    mm = nc.tensor.transpose(ps[:, h, P * t:P * (t + 1)],
                                             n_sb[:, h % 2, P * t:P * (t + 1)], ident[:])
                mm.then_inc(cat_done, 1)

            def out_part(j, ks):
                for k in ks:
                    if j < 2:
                        pe.wait_ge(cat_ready, cat_count(k))
                    mm = weights_still(ps[:, U_BANK[j % 4], :], j % SLOTS, k, cat_hi[:, k, :],
                                       cat_lo[:, k, :], k == CAT_FIRST[0], k == CAT_LAST[0])
                    if k == CAT_LAST[0]:
                        mm.then_inc(unit_done, 1)

            pe.wait_ge(setup_done, 1)
            gate_up(0, 0, NORM_FFN[0])
            with pe.Fori(1, KF // 2) as i:
                gate_up(0, i)
            with pe.Fori(0, 2) as i:
                down_tiles(i)

            pe.wait_ge(x_updated, 5)
            for m in range(4):
                if m:
                    pe.wait_ge(x_updated, 5 + m)
                column_tile(MIX0 + QK0 + m, m, m, NORM_MIX if m == 0 else None)
                if m == 0:
                    mean_square(NORM_MIX)
                    for t in range(TT):
                        mm = nc.tensor.matmul(ps[:, TOK_BANK, t:t + 1],
                                              ssq[:, 0, P * t:P * (t + 1)], mean_w[:, 0:1],
                                              start=True, stop=True)
                    mm.then_inc(tok_mean_done, 1)
            pe.wait_ge(rms_ready, NORM_MIX + 1)
            pe.wait_ge(tok_rms_ready, 1)
            for c in token_tiles(MIX0 + V0, 4):
                pass
            pe.wait_ge(rot_ready, 4)
            for h in token_tiles(MIX0 + G0, 0):
                if h == 0:
                    pe.wait_ge(v_ready, TT)
                    pe.wait_ge(qk_ready, 4)
                else:
                    pe.wait_ge(pt_ready, h)
                scores(h)
            for s in range(4):
                if s == 1:
                    pe.wait_ge(pt_ready, HEADS)
                column_tile(MIX0 + U0 + s, s, U_BANK[s])
                if s == 0:
                    pe.wait_ge(sg_ready, TT)
                    pe.wait_ge(pt_ready, HEADS)
                attend(s)
                for event in CAT_AFTER[s]:
                    (pooled_product if event[0] == "y" else turn)(int(event[1]))
            for j in range(2):
                pe.wait_ge(lo_split, MIX0 + O0 + j + 1)
            out_part(0, CAT_FIRST)
            turn(2)
            out_part(1, CAT_FIRST)
            pooled_product(3)
            turn(3)
            for ks in (CAT_NEXT, CAT_LAST):
                for j in range(2):
                    out_part(j, ks)
            for j in range(2, KD):
                pe.wait_ge(lo_split, MIX0 + O0 + j + 1)
                if j >= 4:
                    pe.wait_ge(x_updated, KD + j - 3)
                out_part(j, CAT_FIRST + CAT_NEXT + CAT_LAST)

            gate_up(1, 0, NORM_FFN[1])
            with pe.Fori(1, KF // 2) as i:
                gate_up(1, i)
            for dh in range(2):
                last_half(dh)

        @block.scalar
        def _(act):
            def split(rnd, c):
                n, s = SLOTS * rnd + c, c % SLOTS
                act.wait_ge(raw_landed[s], 16 * (rnd + c // SLOTS + 1))
                if known(n, SLOTS):
                    act.wait_ge(unit_done, n - SLOTS + 1)
                nc.scalar.activation(w_hi[:, s, :], w_raw[:, s, :], ACT.Copy).then_inc(hi_split, 1)

            def hi_of_h(norm, j):
                nc.scalar.activation(at(h_hi, j), at(x, j), ACT.Copy,
                                     scale=gain[:, bass.ds(GAIN_NORM[norm] + j, 1)]
                                     ).then_inc(h_hi_ready, 1)

            def square_of(norm, j, b):
                act.wait_ge(ssq_added, added(norm, j) - 2)
                nc.scalar.activation(at(square, b), at(x, j), ACT.Square
                                     ).then_inc(square_ready, 1)

            def first_square(j):
                if j >= 4:
                    act.wait_ge((ssq_added, odd_added)[j % 2], j // 2 - 1)
                nc.scalar.activation((ssq, rms)[j][:, 0, :] if j < 2 else square[:, j % 2, :],
                                     x[:, j, :], ACT.Square).then_inc(square_ready, 1)

            def next_norm(norm, j, b):
                act.wait_ge(x_updated, KD * (norm - 1) + j + 1)
                hi_of_h(norm, j)
                square_of(norm, j, b)

            def take_rms(norm):
                act.wait_ge(mean_done, norm + 1)
                nc.scalar.activation(rms[:, 0, :], ps[:, NORM_BANK, :], ACT.Sqrt,
                                     bias=eps[:, 0:1]).then_inc(rms_ready, 1)

            def activate(f, i, m):
                ft = KF * f + 2 * i + m
                act.wait_ge(gate_scaled, ft + 1)
                nc.scalar.activation(tmp_a[:, 0, :], tmp_a[:, 0, :], ACT.Silu
                                     ).then_inc(silu_ready, 1)

            def gate_up(f, i, norm=None):
                for m in range(2):
                    split(rounds(GU0[f]) + i, 2 * m + AHEAD)
                    split(rounds(GU0[f]) + i, 2 * m + AHEAD + 1)
                    if m == 0 and norm is not None:
                        take_rms(norm)
                    activate(f, i, m)

            def down_tiles(i):
                for j in range(4):
                    for c in range(3 * j + AHEAD, 3 * j + 3 + AHEAD):
                        split(rounds(DOWN0[0]) + 3 * i, c)
                    next_norm(NORM_MIX, 4 * i + j, j % 2)

            def last_sums(dh, t):
                wait_last_tile(act, dh, t)
                if dh or t:
                    act.wait_ge(last_square, TT * dh + t)
                nc.scalar.activation(square[:, 0, :], ps[:, TT * (1 - dh) + t, :], ACT.Square,
                                     accum_out=last_sum[:, dh, t:t + 1]).then_inc(last_square, 1)

            def hi_of_cat(event):
                bank, k, g = cat_place(event)
                act.wait_ge(cat_done, CAT_EVENTS.index(event) + 1)
                nc.scalar.activation(cat_hi[:, k, :], ps[:, bank, :], ACT.Copy,
                                     scale=gain[:, g:g + 1]).then_inc(cat_hi_ready, 1)

            def group_std(h):
                act.wait_ge(var_ready, h + 1)
                nc.scalar.activation(gn_std[:], meanvar[:, :, 1], ACT.Sqrt,
                                     bias=eps[:, 1:2]).then_inc(gn_std_ready, 1)

            act.dma_start(gain[:], gains).then_inc(gain_landed, 16)
            act.dma_start(rope_sb[:], rope).then_inc(rope_landed, 16)
            act.wait_ge(setup_done, 1)
            nc.scalar.activation(warm[:], eps[:, 0:1], ACT.Sqrt)

            half = UNIT // 2
            act.wait_ge(half_landed, 16)
            nc.scalar.activation(w_hi[:, 0, 0:half], w_raw[:, 0, 0:half], ACT.Copy
                                 ).then_inc(half_hi_split, 1)
            act.wait_ge(gain_landed, 16)
            for j in range(KD):
                if j % 2 == 0:
                    act.wait_ge(x_landed[j // 2], 16)
                hi_of_h(NORM_FFN[0], j)
                if j == 1:
                    act.wait_ge(raw_landed[0], 16)
                    nc.scalar.activation(w_hi[:, 0, half:UNIT], w_raw[:, 0, half:UNIT], ACT.Copy
                                         ).then_inc(hi_split, 1)
            split(0, 1)
            for j in range(KD):
                first_square(j)
            gate_up(0, 0, NORM_FFN[0])
            with act.Fori(1, KF // 2) as i:
                gate_up(0, i)
            for i in range(2):
                down_tiles(i)

            for n in range(MIX_UNITS):
                split(rounds(MIX0), n + AHEAD)
                if n == QK0:
                    take_rms(NORM_MIX)
                    act.wait_ge(tok_mean_done, 1)
                    nc.scalar.activation(rms_tok[:], ps[:, TOK_BANK, 0:TT], ACT.Sqrt,
                                         bias=eps[:, 0:1]).then_inc(tok_rms_ready, 1)
                if n == V0 + 3:
                    act.wait_ge(tok_rstd_ready, 1)
                    act.wait_ge(unit_done, MIX0 + n + 1)
                    for t in range(TT):
                        nc.scalar.activation(v[:, t, :], ps[:, 4 + t, :], ACT.Copy,
                                             scale=rstd_tok[:, t:t + 1]).then_inc(v_ready, 1)
                if n == G0 + 3:
                    act.wait_ge(unit_done, MIX0 + n + 1)
                    for t in range(TT):
                        nc.scalar.activation(sg[:, t, :], ps[:, t, :], ACT.Silu,
                                             scale=rstd_tok[:, t:t + 1]).then_inc(sg_ready, 1)
                if U0 <= n < O0:
                    for task, arg in RET_TASKS[n - U0]:
                        if task == "cat":
                            hi_of_cat(arg)
                        if task == "stats":
                            group_std(arg)
                if n >= O0:
                    next_norm(NORM_FFN[1], n - O0, n % 2)

            gate_up(1, 0, NORM_FFN[1])
            with act.Fori(1, KF // 2) as i:
                gate_up(1, i)
            for c in range(2 * LAST_UNITS):
                if c == LAST_UNITS - 1:
                    for t in range(TT - 1):
                        last_sums(0, t)
                if c + AHEAD < 2 * LAST_UNITS:
                    split(rounds(DOWN0[1]), c + AHEAD)
                if c == LAST_UNITS - 1:
                    last_sums(0, TT - 1)
            nc.scalar.activation(warm[:], eps[:, 0:1], ACT.Sqrt)
            for t in range(TT):
                last_sums(1, t)
                if t == 0:
                    act.wait_ge(last_bias_ready, 1)
                act.wait_ge(last_square, TT + t + 1)
                nc.scalar.activation(rms_tok[:, t:t + 1], last_sum[:, 1, t:t + 1], ACT.Sqrt,
                                     bias=last_bias[:, t:t + 1], scale=1.0 / D
                                     ).then_inc(last_rms_ready, 1)

        @block.vector
        def _(dve):
            def split(rnd, c):
                n, s = SLOTS * rnd + c, c % SLOTS
                dve.wait_ge(hi_split, n + 1)
                nc.vector.tensor_tensor(w_lo[:, s, :], w_raw[:, s, :],
                                        w_hi[:, s, :].bitcast(F32), ALU.subtract
                                        ).then_inc(lo_split, 1)

            def lo_of_h(norm, j):
                dve.wait_ge(h_hi_ready, KD * norm + j + 1)
                nc.vector.scalar_tensor_tensor(
                    out=at(h_lo, j), in0=at(x, j),
                    scalar=gain[:, bass.ds(GAIN_NORM[norm] + j, 1)],
                    in1=at(h_hi, j).bitcast(F32), op0=ALU.mult, op1=ALU.subtract
                    ).then_inc(h_ready, 1)

            def update_x(norm, j, bank, n):
                dve.wait_ge(unit_done, n + 1)
                nc.vector.tensor_tensor(at(x, j), at(ps, bank), at(x, j), ALU.add
                                        ).then_inc(x_updated, 1)
                lo_of_h(norm, j)

            def take_rstd(norm):
                dve.wait_ge(rms_ready, norm + 1)
                nc.vector.reciprocal(rstd[:, 0, :], rms[:, 0, :]).then_inc(rstd_ready, 1)

            def activate(f, i, m):
                ft = KF * f + 2 * i + m
                n = GU0[f] + 4 * i + 2 * m
                dve.wait_ge(unit_done, n + 1)
                nc.vector.tensor_tensor(tmp_a[:, 0, :], ps[:, 2 * m, :], rstd[:, 0, :], ALU.mult
                                        ).then_inc(gate_scaled, 1)
                dve.wait_ge(unit_done, n + 2)
                if known(ft, 1):
                    dve.wait_ge(a_lo_ready, ft)
                nc.vector.scalar_tensor_tensor(out=tmp_b[:, 0, :], in0=ps[:, 2 * m + 1, :],
                                               scalar=0.5, in1=rstd[:, 0, :],
                                               op0=ALU.mult, op1=ALU.mult).then_inc(up_scaled, 1)
                dve.wait_ge(up_scaled, ft + 1)
                dve.wait_ge(silu_ready, ft + 1)
                nc.vector.tensor_tensor(at(a_hi, 2 * i + m), tmp_a[:], tmp_b[:], ALU.mult)
                nc.vector.tensor_tensor(tmp_b[:], tmp_a[:], tmp_b[:], ALU.mult).then_inc(a_ready, 1)
                dve.wait_ge(a_ready, ft + 1)
                nc.vector.tensor_tensor(at(a_lo, 2 * i + m), at(tmp_b, 0),
                                        at(a_hi, 2 * i + m).bitcast(F32), ALU.subtract
                                        ).then_inc(a_lo_ready, 1)

            def gate_up(f, i, norm=None):
                for m in range(2):
                    split(rounds(GU0[f]) + i, 2 * m + AHEAD)
                    split(rounds(GU0[f]) + i, 2 * m + AHEAD + 1)
                    if m == 0 and norm is not None:
                        take_rstd(norm)
                        dve.wait_ge(rstd_ready, norm + 1)
                    activate(f, i, m)

            def down_tiles(i):
                for j in range(4):
                    for c in range(3 * j + AHEAD, 3 * j + 3 + AHEAD):
                        split(rounds(DOWN0[0]) + 3 * i, c)
                    update_x(NORM_MIX, 4 * i + j, 4 - 4 * i + j, DOWN0[0] + 12 * i + 3 * j + 2)

            def last_gains(dh, t):
                dve.wait_ge(last_square, TT * dh + t + 1)
                nc.vector.tensor_tensor(x[:, TT * dh + t, :], ps[:, TT * (1 - dh) + t, :],
                                        rope_sb[:, dh, :], ALU.mult).then_inc(last_gained, 1)

            def rotate(m):
                dve.wait_ge(unit_done, MIX0 + QK0 + m + 1)
                if m:
                    dve.wait_ge(qk_ready, m)
                nc.vector.tensor_tensor(rot_a[:, 0, :], ps[:, m, :], tmp_a[:, 0, :], ALU.mult)
                for src in range(0, P, DK // 2):
                    dst = src ^ (DK // 2)
                    last = nc.vector.tensor_tensor(rot_b[dst:dst + DK // 2, 0, :],
                                                   ps[src:src + DK // 2, m, :],
                                                   tmp_b[src:src + DK // 2, 0, :], ALU.mult)
                last.then_inc(rot_ready, 1)

            def decay_scores(h):
                dve.wait_ge(scores_done, h + 1)
                for j, (bank, col) in enumerate(SCORE_AT):
                    w = T - P * j
                    last = nc.vector.tensor_tensor(pt[:, h, PT_AT[j]:PT_AT[j] + w],
                                                   ps[:, bank, col:col + w],
                                                   decay_sb[:, h, 0:w], ALU.mult)
                last.then_inc(pt_ready, 1)

            def take_u(s):
                dve.wait_ge(unit_done, MIX0 + U0 + s + 1)
                if s >= 2:
                    dve.wait_ge(cat_done, CAT_EVENTS.index(f"y{s - 2}") + 1)
                nc.vector.tensor_tensor(u_sb[:, s % 2, :], ps[:, U_BANK[s], :], rstd[:, 0, :],
                                        ALU.mult).then_inc(u_ready, 1)

            def window_mean(s):
                w = WINDOWS[3 - s]
                levels = w.bit_length() - 1
                total = (rot_a, rot_b)[(levels - 1) % 2]
                dve.wait_ge(sum_ready, s + 1)
                nc.vector.tensor_tensor(total[:, 0, 0:16], total[:, 0, 0:16], edge_sb[:, 3 - s, :],
                                        ALU.mult).then_inc(edge_done, 1)
                dve.wait_ge(edge_done, s + 1)
                nc.vector.scalar_tensor_tensor(out=u_sb[:, s % 2, :], in0=total[:, 0, :],
                                               scalar=1.0 / w, in1=u_sb[:, s % 2, :],
                                               op0=ALU.mult, op1=ALU.subtract
                                               ).then_inc(pooled_ready, 1)

            def group_stats(h):
                dve.wait_ge(pv_done, h + 1)
                for t in range(TT):
                    last = nc.vector.bn_stats(stats[:, t, :], ps[:, h, P * t:P * (t + 1)])
                last.then_inc(stats_ready, 1)
                dve.wait_ge(stats_ready, h + 1)
                for t in range(TT):
                    last = nc.vector.bn_aggr(meanvar[:, t, :], stats[:, t, :])
                last.then_inc(var_ready, 1)

            def group_norm(h):
                dve.wait_ge(gn_std_ready, h + 1)
                nc.vector.reciprocal(gn_rstd[:], gn_std[:]).then_inc(gn_rstd_ready, 1)
                dve.wait_ge(gn_rstd_ready, h + 1)
                if h >= 2:
                    dve.wait_ge(cat_done, CAT_EVENTS.index(f"t{h - 2}") + 1)
                for t in range(TT):
                    last = nc.vector.tensor_scalar(n_sb[:, h % 2, P * t:P * (t + 1)],
                                                   ps[:, h, P * t:P * (t + 1)],
                                                   meanvar[:, t, 0:1], gn_rstd[:, t:t + 1],
                                                   ALU.subtract, ALU.mult)
                last.then_inc(gn_scaled, 1)
                dve.wait_ge(gn_scaled, h + 1)
                n3 = n_sb[:, h % 2, :].rearrange("p (t c) -> p t c", t=TT)
                nc.vector.tensor_tensor(n3, n3, sg[:, :, DV * h:DV * (h + 1)], ALU.mult
                                        ).then_inc(ret_ready, 1)

            def lo_of_cat(event):
                bank, k, g = cat_place(event)
                dve.wait_ge(cat_hi_ready, CAT_EVENTS.index(event) + 1)
                nc.vector.scalar_tensor_tensor(out=cat_lo[:, k, :], in0=ps[:, bank, :],
                                               scalar=gain[:, g:g + 1],
                                               in1=cat_hi[:, k, :].bitcast(F32),
                                               op0=ALU.mult, op1=ALU.subtract
                                               ).then_inc(cat_ready, 1)

            half = UNIT // 2
            dve.wait_ge(half_hi_split, 1)
            nc.vector.tensor_tensor(w_lo[:, 0, 0:half], w_raw[:, 0, 0:half],
                                    w_hi[:, 0, 0:half].bitcast(F32), ALU.subtract
                                    ).then_inc(half_split, 1)
            for j in range(KD):
                lo_of_h(NORM_FFN[0], j)
                if j == 1:
                    dve.wait_ge(hi_split, 1)
                    nc.vector.tensor_tensor(w_lo[:, 0, half:UNIT], w_raw[:, 0, half:UNIT],
                                            w_hi[:, 0, half:UNIT].bitcast(F32), ALU.subtract
                                            ).then_inc(lo_split, 1)
            split(0, 1)
            for j in range(3, KD, 2):
                dve.wait_ge(square_ready, j + 1)
                if j > 3:
                    dve.wait_ge(odd_added, j // 2 - 1)
                nc.vector.tensor_tensor(rms[:, 0, :], rms[:, 0, :], square[:, 1, :], ALU.add
                                        ).then_inc(odd_added, 1)
            gate_up(0, 0, NORM_FFN[0])
            with dve.Fori(1, KF // 2) as i:
                gate_up(0, i)
            with dve.Fori(0, 2) as i:
                down_tiles(i)

            for n in range(MIX_UNITS):
                split(rounds(MIX0), n + AHEAD)
                if n == QK0:
                    take_rstd(NORM_MIX)
                    dve.wait_ge(tok_rms_ready, 1)
                    nc.vector.reciprocal(rstd_tok[:], rms_tok[:]).then_inc(tok_rstd_ready, 1)
                    dve.wait_ge(rstd_ready, NORM_MIX + 1)
                    dve.wait_ge(rope_landed, 16)
                    for r, t in enumerate((tmp_a, tmp_b)):
                        nc.vector.tensor_tensor(t[:, 0, :], rope_sb[:, r, :], rstd[:, 0, :],
                                                ALU.mult).then_inc(rope_scaled, 1)
                    dve.wait_ge(rope_scaled, 2)
                if n < V0:
                    rotate(n)
                if G0 <= n < U0:
                    if n == G0:
                        dve.wait_ge(mix_landed, 48)
                    decay_scores(n - G0)
                if U0 <= n < O0:
                    for task, arg in RET_TASKS[n - U0]:
                        {"u": take_u, "mean": window_mean, "stats": group_stats,
                         "norm": group_norm, "cat": lo_of_cat}[task](arg)
                if n >= O0:
                    update_x(NORM_FFN[1], n - O0, U_BANK[(n - O0) % 4], MIX0 + n)

            gate_up(1, 0, NORM_FFN[1])
            with dve.Fori(1, KF // 2) as i:
                gate_up(1, i)
            dve.wait_ge(last_gain_landed, 16)
            for c in range(2 * LAST_UNITS):
                if c == LAST_UNITS - 1:
                    for t in range(TT - 1):
                        last_gains(0, t)
                if c + AHEAD < 2 * LAST_UNITS:
                    split(rounds(DOWN0[1]), c + AHEAD)
                if c == LAST_UNITS - 1:
                    last_gains(0, TT - 1)
                    nc.vector.tensor_scalar(last_bias[:], last_sum[:, 0, :], 1.0 / D, RMS_EPS,
                                            ALU.mult, ALU.add).then_inc(last_bias_ready, 1)
            for t in range(TT):
                last_gains(1, t)
                dve.wait_ge(last_rms_ready, t + 1)
                nc.vector.reciprocal(rstd_tok[:, t:t + 1], rms_tok[:, t:t + 1]
                                     ).then_inc(last_rstd_ready, 1)
                dve.wait_ge(last_rstd_ready, t + 1)
                dve.wait_ge(last_gained, TT + t + 1)
                for dh in range(2):
                    nc.vector.tensor_scalar(x[:, TT * dh + t, :], x[:, TT * dh + t, :],
                                            rstd_tok[:, t:t + 1], None, ALU.mult
                                            ).then_inc(y_ready, 1)

        @block.gpsimd
        def _(pool):
            def sum_squares(norm, j, b):
                pool.wait_ge(square_ready, KD * norm + j + 1)
                pool.wait_ge(ssq_added, added(norm, j) - 1)
                nc.gpsimd.tensor_tensor(ssq[:, 0, :], ssq[:, 0, :], square[:, b, :], ALU.add
                                        ).then_inc(ssq_added, 1)

            def clear_squares(norm):
                pool.wait_ge(mean_done, norm)
                if norm == NORM_MIX + 1:
                    pool.wait_ge(tok_mean_done, 1)
                nc.gpsimd.memset(ssq[:], 0.0).then_inc(ssq_cleared, 1)
                pool.wait_ge(ssq_cleared, norm)

            def window_sums(s):
                pool.wait_ge(u_ready, s + 1)
                if s:
                    pool.wait_ge(pooled_ready, s)
                src, d, l = u_sb[:, s % 2, :], 1, 0
                while d < WINDOWS[3 - s]:
                    dst = (rot_a, rot_b)[l % 2][:, 0, :]
                    nc.gpsimd.tensor_copy(dst[:, 0:d], src[:, 0:d])
                    add = nc.gpsimd.tensor_tensor(dst[:, d:T], src[:, d:T], src[:, 0:T - d],
                                                  ALU.add)
                    src, d, l = dst, 2 * d, l + 1
                    if d < WINDOWS[3 - s]:
                        add.then_inc(sum_step, 1)
                        pool.wait_ge(sum_step, SUM_STEPS[s] + l)
                add.then_inc(sum_ready, 1)

            nc.gpsimd.memset(mean_w[:], 1.0 / D)
            nc.gpsimd.memset(eps[:, 0:1], RMS_EPS)
            nc.gpsimd.memset(eps[:, 1:2], GN_EPS)
            nc.gpsimd.memset(ident[:], 0.0).then_inc(setup_step, 1)
            pool.wait_ge(setup_step, 1)
            nc.gpsimd.affine_select(out=ident[:], in_=ident[:], compare_op=ALU.not_equal, fill=1.0,
                                    base=0, pattern=[[-1, P]], channel_multiplier=1
                                    ).then_inc(setup_done, 1)

            for j in range(2, KD, 2):
                pool.wait_ge(square_ready, j + 1)
                if j > 2:
                    pool.wait_ge(ssq_added, j // 2 - 1)
                nc.gpsimd.tensor_tensor(ssq[:, 0, :], ssq[:, 0, :], square[:, 0, :], ALU.add
                                        ).then_inc(ssq_added, 1)
            pool.wait_ge(ssq_added, 3)
            pool.wait_ge(odd_added, 3)
            nc.gpsimd.tensor_tensor(ssq[:, 0, :], ssq[:, 0, :], rms[:, 0, :], ALU.add
                                    ).then_inc(ssq_added, 1)
            clear_squares(NORM_MIX)
            with pool.Fori(0, KD // 2) as i:
                for b in range(2):
                    sum_squares(NORM_MIX, 2 * i + b, b)
            for m in range(4):
                pool.wait_ge(rot_ready, m + 1)
                nc.gpsimd.tensor_tensor(qk[:, m, :], rot_a[:, 0, :], rot_b[:, 0, :], ALU.add
                                        ).then_inc(qk_ready, 1)
            for s in range(4):
                window_sums(s)
            clear_squares(NORM_FFN[1])
            with pool.Fori(0, KD // 2) as i:
                for b in range(2):
                    sum_squares(NORM_FFN[1], 2 * i + b, b)


def decay_table():
    gamma = 1.0 - 2.0 ** (-5.0 - np.arange(HEADS))
    key, query = np.arange(P)[:, None], np.arange(T)[None, :]
    seen = query // CHUNK >= key // CHUNK
    dist = np.abs(query - key)
    return np.stack([np.where(seen, g ** dist, 0.0) * DK ** -0.5 for g in gamma],
                    axis=1).astype(np.float32)


def rope_table():
    half = DK // 2
    f = np.arange(P) % half
    freq = (ROPE_BASE ** (-f * 2.0 / DK)).astype(np.float32)
    ang = (np.arange(T, dtype=np.float32)[None, :] * freq[:, None]).astype(np.float64)
    sign = np.where(np.arange(P) % DK < half, 1.0, -1.0)[:, None]
    return np.stack([np.cos(ang), sign * np.sin(ang)], axis=1).astype(np.float32)


def edge_table():
    t = np.arange(16) + 1
    rows = np.stack([w / np.minimum(t, w) for w in WINDOWS])
    return np.broadcast_to(rows, (P,) + rows.shape).astype(np.float32).copy()


def kernel(**inputs):
    import concourse.bacc as bacc
    from concourse.bass_utils import run_bass_kernel_spmd

    w = {k: np.asarray(a) for k, a in inputs.items()}

    def columns(a):
        k, m = a.shape
        return np.ascontiguousarray(a.reshape(k // P, P, m // P, P).transpose(2, 1, 0, 3)
                                    .reshape(m // P, P, k))

    def k_pairs(a):
        return a.reshape(4, 2, P, T).transpose(0, 2, 1, 3).reshape(4, P, 2 * T)

    def by_feature(a):
        return a.reshape(-1, P).T

    w_in = w["w_in"][0]
    qk_cols, v_end, g_end = 2 * HEADS * DK, 2 * HEADS * DK + HEADS * DV, 2 * HEADS * (DK + DV)
    arrays = {
        "xT": np.ascontiguousarray(w["x"][0].T.reshape(KD, P, T).transpose(1, 0, 2)),
        "gate": columns(w["ffn1_gate"][0]), "up": columns(w["ffn1_up"][0]),
        "down": columns(w["ffn1_down"][0]),
        "gate2": columns(w["ffn2_gate"][0]), "up2": columns(w["ffn2_up"][0]),
        "down2": np.ascontiguousarray(w["ffn2_down"][0].reshape(LAST_UNITS, 2, P, 2, T)
                                      .transpose(3, 0, 2, 1, 4).reshape(2 * LAST_UNITS, P, UNIT)),
        "w_qku": np.concatenate([columns(w_in[:, :qk_cols]), columns(w_in[:, g_end:])]),
        "w_vg": np.concatenate([k_pairs(w_in[:, qk_cols:v_end]), k_pairs(w_in[:, v_end:g_end])]),
        "w_out": columns(w["w_out"][0]),
        "pool_w": np.ascontiguousarray(w["pool_w"][0].transpose(1, 0, 2)),
        "gains": np.ascontiguousarray(np.concatenate(
            [by_feature(a) for a in (w["norm_ffn1"], w["norm_mix"], w["norm_ffn2"],
                                     w["ret_gn_gain"], w["pool_scale"])], axis=1)),
        "last_gain": w["norm_final"],
        "decay": decay_table(), "rope": rope_table(), "edge": edge_table(),
    }
    nc = bacc.Bacc("TRN2", target_bir_lowering=False, num_devices=1)
    args = [nc.dram_tensor(f"{n}_dram", a.shape, mybir.dt.from_np(a.dtype),
                           kind="ExternalInput").ap() for n, a in arrays.items()]
    args.append(nc.dram_tensor("out_dram", (T, D), F32, kind="ExternalOutput").ap())
    program(nc, *args)
    r = run_bass_kernel_spmd(nc, [{f"{n}_dram": a for n, a in arrays.items()}], core_ids=[0])
    return r.results[0]["out_dram"][None]
```

```python
from contextlib import ExitStack

import numpy as np

import concourse.bass as bass
from concourse import mybir

F32 = mybir.dt.float32
F32R = mybir.dt.float32r
ACT = mybir.ActivationFunctionType
ALU = mybir.AluOpType

P = 128
D = 1024
T = 512
FF = 2816
KD = D // P
KF = FF // P
TT = T // P
HEADS = 4
DK = 64
DV = 128
CHUNK = 64
WINDOWS = (2, 4, 8, 16)
RMS_EPS = 1e-6
GN_EPS = 1e-5
ROPE_BASE = 10000.0

SLOTS = 4
UNIT = 1024
AHEAD = 2
DOWN_PARTS = ((0, 8), (8, 15), (15, 22))
LAST_UNITS = KF // 2
START = (("first", 0), ("x", 0), ("first", 1), ("x", 1), ("second", 0), ("x", 2), ("second", 1),
         ("x", 3), ("x", 4), ("x", 5), ("x", 6), ("x", 7))
LAST_JOINT = 3

GU_UNITS = 2 * KF
DOWN_UNITS = len(DOWN_PARTS) * KD
MIX_UNITS = 24
GU0 = (0, GU_UNITS + DOWN_UNITS + MIX_UNITS)
DOWN0 = (GU0[0] + GU_UNITS, GU0[1] + GU_UNITS)
MIX0 = DOWN0[0] + DOWN_UNITS
QK0, V0, G0, U0, O0 = 0, 4, 8, 12, 16

GAIN_NORM = (0, 8, 16)
GAIN_RET = 24
GAIN_POOL = 28
GAINS = 32

NORM_FFN = (0, 2)
NORM_MIX = 1

SCORE_AT = ((4, 0), (5, 0), (6, 0), (5, 384))
PT_AT = (0, 512, 896, 1152)
PT = 1280
CAT_FIRST, CAT_NEXT, CAT_LAST = (7, 6, 0, 5, 1), (4, 2), (3,)
U_BANK = (7, 4, 5, 6)
NORM_BANK, TOK_BANK = 4, 5

CAT_EVENTS = ("y0", "y1", "t0", "y2", "t1", "t2", "y3", "t3")
CAT_AFTER = ((), ("y0",), ("y1", "t0"), ("y2", "t1"))
RET_TASKS = (
    (("u", 0), ("stats", 0), ("norm", 0), ("mean", 0)),
    (("u", 1), ("stats", 1), ("norm", 1), ("mean", 1), ("cat", "y0")),
    (("u", 2), ("stats", 2), ("cat", "y1"), ("cat", "t0"), ("norm", 2), ("mean", 2)),
    (("u", 3), ("mean", 3), ("cat", "y2"), ("cat", "t1"), ("stats", 3), ("norm", 3),
     ("cat", "t2"), ("cat", "y3"), ("cat", "t3")),
)
SUM_STEPS = (0, 3, 5, 6)


def cat_place(event):
    n = int(event[1])
    if event[0] == "y":
        return U_BANK[n], HEADS + 3 - n, GAIN_POOL + 3 - n
    return n, n, GAIN_RET + n


def added(norm, j):
    return 4 + KD * (norm - 1) + j + 1 if norm else 4


def cat_count(k):
    return 1 + [cat_place(e)[1] for e in CAT_EVENTS].index(k)


def program(nc, xT, gate, up, down, gate2, up2, down2, w_qku, w_vg, w_out, pool_w, gains,
            last_gain, decay, rope, edge, out):
    with ExitStack() as ctx:
        def sb(name, shape, dt=F32, scope=ctx):
            return scope.enter_context(nc.sbuf_tensor(name, shape, dt))

        def sem(name):
            return ctx.enter_context(nc.semaphore(name))

        x = sb("x_sb", [P, KD, T])
        h_hi = sb("h_hi", [P, KD, T], F32R)
        h_lo = sb("h_lo", [P, KD, T], F32R)
        w_raw = sb("w_raw", [P, SLOTS, UNIT])
        w_hi = sb("w_hi", [P, SLOTS, UNIT], F32R)
        w_lo = sb("w_lo", [P, SLOTS, UNIT], F32R)
        rstd = sb("rstd", [P, 1, T])
        rms = sb("rms", [P, 1, T])
        ssq = sb("ssq", [P, 1, T])
        square = sb("square", [P, 2, T])
        tmp_a = sb("tmp_a", [P, 1, T])
        tmp_b = sb("tmp_b", [P, 1, T])
        gain = sb("gain", [P, GAINS])
        rope_sb = sb("rope_sb", [P, 2, T])
        mean_w = sb("mean_w", [P, P])
        eps = sb("eps", [P, 2])
        rms_tok = sb("rms_tok", [P, TT])
        rstd_tok = sb("rstd_tok", [P, TT])
        ident = sb("ident", [P, P])
        warm = sb("warm", [P, 1])
        last_sum = sb("last_sum", [P, 2, TT])
        last_bias = sb("last_bias", [P, TT])
        stats = sb("stats", [P, TT, 6])
        meanvar = sb("meanvar", [P, TT, 2])
        gn_std = sb("gn_std", [P, TT])
        gn_rstd = sb("gn_rstd", [P, TT])

        with ExitStack() as ffn_scope:
            a_hi = sb("a_hi", [P, KF, T], F32R, ffn_scope)
            a_lo = sb("a_lo", [P, KF, T], F32R, ffn_scope)
        with ExitStack() as mix_scope:
            qk = sb("qk", [P, 4, T], scope=mix_scope)
            v = sb("v", [P, TT, HEADS * DV], scope=mix_scope)
            pt = sb("pt", [P, HEADS, PT], scope=mix_scope)
            sg = sb("sg", [P, TT, HEADS * DV], scope=mix_scope)
            cat_hi = sb("cat_hi", [P, KD, T], F32R, mix_scope)
            cat_lo = sb("cat_lo", [P, KD, T], F32R, mix_scope)
            decay_sb = sb("decay_sb", [P, HEADS, T], scope=mix_scope)
            pool_w_sb = sb("pool_w_sb", [P, HEADS, P], scope=mix_scope)
            edge_sb = sb("edge_sb", [P, len(WINDOWS), 16], scope=mix_scope)
            rot_a = sb("rot_a", [P, 1, T], scope=mix_scope)
            rot_b = sb("rot_b", [P, 1, T], scope=mix_scope)
        q_pair, k_pair, k_lo = cat_hi[:, 0:HEADS, :], cat_hi[:, HEADS:KD, :], cat_lo[:, 0:HEADS, :]
        u_sb = qk[:, 0:2, :]
        n_sb = qk[:, 2:4, :]

        ps = ctx.enter_context(nc.psum_tensor("ps", [P, 8, T], F32))

        raw_landed = [sem(f"raw_landed{s}") for s in range(SLOTS)]
        hi_split = sem("hi_split")
        lo_split = sem("lo_split")
        unit_done = sem("unit_done")
        x_landed = [sem(f"x_landed{k}") for k in range(KD)]
        first_landed = [sem(f"first_landed{c}") for c in range(2)]
        first_hi_split = sem("first_hi_split")
        first_split = sem("first_split")
        gain_landed = sem("gain_landed")
        rope_landed = sem("rope_landed")
        mix_landed = sem("mix_landed")
        eps_set = sem("eps_set")
        setup_step = sem("setup_step")
        setup_done = sem("setup_done")
        x_updated = sem("x_updated")
        h_hi_ready = sem("h_hi_ready")
        h_ready = sem("h_ready")
        square_ready = sem("square_ready")
        ssq_cleared = sem("ssq_cleared")
        ssq_added = sem("ssq_added")
        odd_added = sem("odd_added")
        mean_done = sem("mean_done")
        rms_ready = sem("rms_ready")
        rstd_ready = sem("rstd_ready")
        tok_mean_done = sem("tok_mean_done")
        tok_rms_ready = sem("tok_rms_ready")
        tok_rstd_ready = sem("tok_rstd_ready")
        gate_scaled = sem("gate_scaled")
        up_scaled = sem("up_scaled")
        silu_ready = sem("silu_ready")
        a_ready = sem("a_ready")
        a_lo_ready = sem("a_lo_ready")
        rope_scaled = sem("rope_scaled")
        rot_ready = sem("rot_ready")
        qk_ready = sem("qk_ready")
        qk_hi_ready = sem("qk_hi_ready")
        qk_split = sem("qk_split")
        v_ready = sem("v_ready")
        sg_ready = sem("sg_ready")
        scores_done = sem("scores_done")
        pt_ready = sem("pt_ready")
        pv_done = sem("pv_done")
        u_ready = sem("u_ready")
        sum_step = sem("sum_step")
        sum_ready = sem("sum_ready")
        edge_done = sem("edge_done")
        pooled_ready = sem("pooled_ready")
        stats_ready = sem("stats_ready")
        var_ready = sem("var_ready")
        gn_std_ready = sem("gn_std_ready")
        gn_rstd_ready = sem("gn_rstd_ready")
        gn_scaled = sem("gn_scaled")
        ret_ready = sem("ret_ready")
        cat_done = sem("cat_done")
        cat_hi_ready = sem("cat_hi_ready")
        cat_ready = sem("cat_ready")
        last_gain_landed = sem("last_gain_landed")
        tile_done = sem("tile_done")
        last_square = sem("last_square")
        last_bias_ready = sem("last_bias_ready")
        last_gained = sem("last_gained")
        last_rms_ready = sem("last_rms_ready")
        last_rstd_ready = sem("last_rstd_ready")
        y_ready = sem("y_ready")
        stored = sem("stored")

        def at(t, i):
            return t[:, bass.ds(i, 1), :]

        def known(n, least):
            return not (isinstance(n, int) and n < least)

        def rounds(n0):
            return n0 // SLOTS

        def splits_beside(m, norm):
            if norm == 0:
                return (4, 5) if m == 0 else ()
            return 2 * m + AHEAD, 2 * m + AHEAD + 1

        def wait_last_tile(engine, dh, t):
            if t < TT - 1:
                engine.wait_ge(tile_done, (TT - 1) * dh + t + 1)
            else:
                engine.wait_ge(unit_done, DOWN0[1] + LAST_UNITS * (dh + 1))

        block = ctx.enter_context(nc.Block())

        @block.sync
        def _(sp):
            def load(rnd, c, src, width=UNIT):
                n, s = SLOTS * rnd + c, c % SLOTS
                if known(n, SLOTS):
                    sp.wait_ge(lo_split, n - SLOTS + 1)
                sp.dma_start(w_raw[:, s, 0:width], src).then_inc(raw_landed[s], 16)

            def load_gate_up(f, i):
                for c in range(4):
                    src = ((gate, up), (gate2, up2))[f][c % 2]
                    load(rounds(GU0[f]) + i, c,
                         src[bass.ds(2 * i + c // 2, 1), :, :].rearrange("a p c -> p (a c)"))

            def load_down(i):
                for j in range(4):
                    for r, (k0, k1) in enumerate(DOWN_PARTS):
                        load(rounds(DOWN0[0]) + 3 * i, 3 * j + r,
                             down[bass.ds(4 * i + j, 1), :, k0 * P:k1 * P]
                             .rearrange("a p c -> p (a c)"), (k1 - k0) * P)

            for step, c in START:
                if step == "x":
                    sp.dma_start(x[:, c, :], xT[:, c, :]).then_inc(x_landed[c], 16)
                    if c == 0:
                        sp.dma_start(gain[:], gains).then_inc(gain_landed, 16)
                else:
                    part, landed = {"first": (slice(0, UNIT // 2), first_landed[c]),
                                    "second": (slice(UNIT // 2, UNIT), raw_landed[c])}[step]
                    sp.dma_start(w_raw[:, c, part], (gate, up)[c][0, :, part]).then_inc(landed, 16)
            for c in range(2, SLOTS):
                load(0, c, (gate, up)[c % 2][c // 2])
            sp.dma_start(rope_sb[:], rope).then_inc(rope_landed, 16)
            with sp.Fori(1, KF // 2) as i:
                load_gate_up(0, i)
            with sp.Fori(0, 2) as i:
                load_down(i)
            units = ([w_qku[m] for m in range(4)] + [w_vg[m] for m in range(8)]
                     + [w_qku[7 - s] for s in range(4)] + [w_out[m] for m in range(KD)])
            for c, src in enumerate(units):
                load(rounds(MIX0), c, src)
                if c == SLOTS:
                    sp.wait_ge(unit_done, MIX0)
                    sp.dma_start(decay_sb[:], decay).then_inc(mix_landed, 16)
                    sp.dma_start(pool_w_sb[:], pool_w).then_inc(mix_landed, 16)
                    sp.dma_start(edge_sb[:], edge).then_inc(mix_landed, 16)
            with sp.Fori(0, KF // 2) as i:
                load_gate_up(1, i)
            sp.wait_ge(rope_scaled, 2)
            sp.dma_start(rope_sb[:].rearrange("p a t -> p (a t)"),
                         last_gain.partition_broadcast(P)).then_inc(last_gain_landed, 16)
            with sp.Fori(0, LAST_UNITS // 2) as i:
                for c in range(4):
                    load(rounds(DOWN0[1]) + i, c, down2[bass.ds(4 * i + c, 1), :, :]
                         .rearrange("a p c -> p (a c)"))
            for c in range(LAST_UNITS // 2 * 4, 2 * LAST_UNITS):
                load(rounds(DOWN0[1]), c, down2[c])

            rows = out.rearrange("(t p) (a c) -> p t a c", p=P, a=2)
            for t in range(TT - 1):
                sp.wait_ge(y_ready, 2 * t + 2)
                sp.dma_start(rows[:, t], x[:, t:KD:TT, :]).then_inc(stored, 16)
            for dh in range(2):
                sp.wait_ge(y_ready, 2 * TT - 1 + dh)
                sp.dma_start(rows[:, TT - 1, dh], x[:, TT * dh + TT - 1, :]).then_inc(stored, 16)
            sp.wait_ge(stored, 16 * (TT + 1))

        @block.tensor
        def _(pe):
            def product(out, pairs, first, last, onto=False):
                for r, (lhs, rhs) in enumerate(pairs):
                    mm = nc.tensor.matmul(out, lhs, rhs, start=first and r == 0,
                                          stop=last and r == 2, skip_group_check=onto)
                return mm

            def weights_still(out, s, c, hi, lo, first, last):
                wh, wl = (w[:, s, c * P:(c + 1) * P] for w in (w_hi, w_lo))
                return product(out, ((wh, hi), (wh, lo), (wl, hi)), first, last)

            def weights_moving(out, s, c, hi, lo, first, last, onto=False):
                wh, wl = (w[:, s, c * T:(c + 1) * T] for w in (w_hi, w_lo))
                return product(out, ((hi, wh), (lo, wh), (hi, wl)), first, last, onto)

            def column_tile(n, s, bank, norm=None):
                pe.wait_ge(lo_split, n + 1)
                for k in range(KD):
                    if norm is not None:
                        pe.wait_ge(h_ready, KD * norm + k + 1)
                    mm = weights_still(ps[:, bank, :], s, k, h_hi[:, k, :], h_lo[:, k, :],
                                       k == 0, k == KD - 1)
                mm.then_inc(unit_done, 1)

            def token_tiles(n0, bank0):
                for c in range(SLOTS):
                    pe.wait_ge(lo_split, n0 + c + 1)
                    for kk in range(2):
                        k = 2 * c + kk
                        for t in range(TT):
                            mm = weights_moving(ps[:, bank0 + t, :], c, kk,
                                                h_hi[:, k, t * P:(t + 1) * P],
                                                h_lo[:, k, t * P:(t + 1) * P],
                                                k == 0, k == KD - 1)
                    mm.then_inc(unit_done, 1)
                    yield c

            def mean_square(norm):
                pe.wait_ge(ssq_added, added(norm, KD - 1))
                nc.tensor.matmul(ps[:, NORM_BANK, :], mean_w[:], ssq[:, 0, :],
                                 start=True, stop=True).then_inc(mean_done, 1)

            def first_pair():
                for k in range(KD):
                    pe.wait_ge(h_ready, k + 1)
                    for c in range(2):
                        if k == 0:
                            pe.wait_ge(first_split, c + 1)
                        if k == KD // 2:
                            pe.wait_ge(lo_split, c + 1)
                        mm = weights_still(ps[:, c, :], c, k, h_hi[:, k, :], h_lo[:, k, :],
                                           k == 0, k == KD - 1)
                        if k == KD - 1:
                            mm.then_inc(unit_done, 1)

            def gate_up(f, i, norm=None):
                for m in range(2):
                    if m == 0 and norm == 0:
                        first_pair()
                        continue
                    ft = KF * f + 2 * i + m
                    n = GU0[f] + 4 * i + 2 * m
                    if known(ft, 2):
                        pe.wait_ge(gate_scaled, ft - 1)
                    column_tile(n, 2 * m, 2 * m, norm if m == 0 else None)
                    if m == 1 and norm == 0:
                        mean_square(norm)
                    if known(ft, 2):
                        pe.wait_ge(up_scaled, ft - 1)
                    column_tile(n + 1, 2 * m + 1, 2 * m + 1)
                    if m == 0 and norm:
                        mean_square(norm)

            def down_tiles(i):
                for j in range(4):
                    for r, (k0, k1) in enumerate(DOWN_PARTS):
                        c = 3 * j + r
                        pe.wait_ge(lo_split, DOWN0[0] + 12 * i + c + 1)
                        pe.wait_ge(a_lo_ready, k1)
                        for k in range(k0, k1):
                            mm = weights_still(at(ps, 4 - 4 * i + j), c % SLOTS, k - k0,
                                               a_hi[:, k, :], a_lo[:, k, :], k == 0, k == KF - 1)
                        mm.then_inc(unit_done, 1)

            def last_half(dh):
                def bank(t):
                    return ps[:, (TT if dh == 0 else 0) + t, :]

                def k_tile(t, c, kk):
                    k = 2 * c + kk
                    return weights_moving(bank(t), (LAST_UNITS * dh + c) % SLOTS, kk,
                                          a_hi[:, k, t * P:(t + 1) * P],
                                          a_lo[:, k, t * P:(t + 1) * P], False, k == KF - 1,
                                          onto=True)

                n0 = DOWN0[1] + LAST_UNITS * dh
                for t in range(TT):
                    for d in range(TT):
                        nc.tensor.matmul(bank(t)[:, P * d:P * (d + 1)],
                                         x[:, TT * dh + d, P * t:P * (t + 1)], ident[:],
                                         is_transpose=True, start=d == 0, stop=False,
                                         skip_group_check=True)
                for c in range(LAST_UNITS - LAST_JOINT):
                    pe.wait_ge(lo_split, n0 + c + 1)
                    pe.wait_ge(a_lo_ready, KF + 2 * c + 2)
                    for kk in range(2):
                        for t in range(TT):
                            mm = k_tile(t, c, kk)
                    mm.then_inc(unit_done, 1)
                pe.wait_ge(lo_split, n0 + LAST_UNITS)
                pe.wait_ge(a_lo_ready, 2 * KF)
                for t in range(TT):
                    for c in range(LAST_UNITS - LAST_JOINT, LAST_UNITS):
                        for kk in range(2):
                            mm = k_tile(t, c, kk)
                        if t == TT - 1:
                            mm.then_inc(unit_done, 1)
                    if t < TT - 1:
                        mm.then_inc(tile_done, 1)

            def scores(h):
                own = slice(DK * (h % 2), DK * (h % 2) + DK)
                for j, (bank, col) in enumerate(SCORE_AT):
                    out_j = ps[:, bank, col:col + T - P * j]
                    nc.tensor.matmul(out_j, k_pair[:, h, P * j:P * (j + 1)], q_pair[:, h, P * j:T],
                                     start=True, stop=False)
                    mm = nc.tensor.matmul(out_j, k_lo[own, h, P * j:P * (j + 1)],
                                          q_pair[own, h, P * j:T], start=False, stop=True)
                mm.then_inc(scores_done, 1)

            def attend(h):
                for i in range(TT):
                    for j in range(i + 1):
                        at_i = PT_AT[j] + P * (i - j)
                        mm = nc.tensor.matmul(ps[:, h, P * i:P * (i + 1)],
                                              pt[:, h, at_i:at_i + P],
                                              v[:, j, DV * h:DV * (h + 1)],
                                              start=j == 0, stop=j == i)
                mm.then_inc(pv_done, 1)

            def pooled_product(s):
                pe.wait_ge(pooled_ready, s + 1)
                nc.tensor.matmul(ps[:, U_BANK[s], :], pool_w_sb[:, 3 - s, :],
                                 u_sb[:, s % 2, :], start=True, stop=True).then_inc(cat_done, 1)

            def turn(h):
                pe.wait_ge(ret_ready, h + 1)
                for t in range(TT):
                    mm = nc.tensor.transpose(ps[:, h, P * t:P * (t + 1)],
                                             n_sb[:, h % 2, P * t:P * (t + 1)], ident[:])
                mm.then_inc(cat_done, 1)

            def out_part(j, ks):
                for k in ks:
                    if j < 2:
                        pe.wait_ge(cat_ready, cat_count(k))
                    mm = weights_still(ps[:, U_BANK[j % 4], :], j % SLOTS, k, cat_hi[:, k, :],
                                       cat_lo[:, k, :], k == CAT_FIRST[0], k == CAT_LAST[0])
                    if k == CAT_LAST[0]:
                        mm.then_inc(unit_done, 1)

            pe.wait_ge(setup_done, 1)
            gate_up(0, 0, NORM_FFN[0])
            with pe.Fori(1, KF // 2) as i:
                gate_up(0, i)
            with pe.Fori(0, 2) as i:
                down_tiles(i)

            pe.wait_ge(x_updated, 5)
            for m in range(4):
                if m:
                    pe.wait_ge(x_updated, 5 + m)
                column_tile(MIX0 + QK0 + m, m, m, NORM_MIX if m == 0 else None)
                if m == 0:
                    mean_square(NORM_MIX)
                    for t in range(TT):
                        mm = nc.tensor.matmul(ps[:, TOK_BANK, t:t + 1],
                                              ssq[:, 0, P * t:P * (t + 1)], mean_w[:, 0:1],
                                              start=True, stop=True)
                    mm.then_inc(tok_mean_done, 1)
            pe.wait_ge(rms_ready, NORM_MIX + 1)
            pe.wait_ge(tok_rms_ready, 1)
            for c in token_tiles(MIX0 + V0, 4):
                pass
            pe.wait_ge(rot_ready, 4)
            for h in token_tiles(MIX0 + G0, 0):
                pe.wait_ge(qk_split, h + 1)
                if h == 0:
                    pe.wait_ge(v_ready, TT)
                else:
                    pe.wait_ge(pt_ready, h)
                scores(h)
            for s in range(4):
                if s == 1:
                    pe.wait_ge(pt_ready, HEADS)
                column_tile(MIX0 + U0 + s, s, U_BANK[s])
                if s == 0:
                    pe.wait_ge(sg_ready, TT)
                    pe.wait_ge(pt_ready, HEADS)
                attend(s)
                for event in CAT_AFTER[s]:
                    (pooled_product if event[0] == "y" else turn)(int(event[1]))
            for j in range(2):
                pe.wait_ge(lo_split, MIX0 + O0 + j + 1)
            out_part(0, CAT_FIRST)
            turn(2)
            pooled_product(3)
            out_part(1, CAT_FIRST)
            turn(3)
            for ks in (CAT_NEXT, CAT_LAST):
                for j in range(2):
                    out_part(j, ks)
            for j in range(2, KD):
                pe.wait_ge(lo_split, MIX0 + O0 + j + 1)
                if j >= 4:
                    pe.wait_ge(x_updated, KD + j - 3)
                out_part(j, CAT_FIRST + CAT_NEXT + CAT_LAST)

            gate_up(1, 0, NORM_FFN[1])
            with pe.Fori(1, KF // 2) as i:
                gate_up(1, i)
            for dh in range(2):
                last_half(dh)

        @block.scalar
        def _(act):
            def split(rnd, c):
                n, s = SLOTS * rnd + c, c % SLOTS
                act.wait_ge(raw_landed[s], 16 * (rnd + c // SLOTS + 1))
                if known(n, SLOTS):
                    act.wait_ge(unit_done, n - SLOTS + 1)
                nc.scalar.activation(w_hi[:, s, :], w_raw[:, s, :], ACT.Copy).then_inc(hi_split, 1)

            def hi_of_h(norm, j):
                nc.scalar.activation(at(h_hi, j), at(x, j), ACT.Copy,
                                     scale=gain[:, bass.ds(GAIN_NORM[norm] + j, 1)]
                                     ).then_inc(h_hi_ready, 1)

            def square_of(norm, j, b):
                act.wait_ge(ssq_added, added(norm, j) - 2)
                nc.scalar.activation(at(square, b), at(x, j), ACT.Square
                                     ).then_inc(square_ready, 1)

            def first_square(j):
                if j >= 4:
                    act.wait_ge((ssq_added, odd_added)[j % 2], j // 2 - 1)
                nc.scalar.activation((ssq, rms)[j][:, 0, :] if j < 2 else square[:, j % 2, :],
                                     x[:, j, :], ACT.Square).then_inc(square_ready, 1)

            def next_norm(norm, j, b):
                act.wait_ge(x_updated, KD * (norm - 1) + j + 1)
                hi_of_h(norm, j)
                square_of(norm, j, b)

            def take_rms(norm):
                act.wait_ge(mean_done, norm + 1)
                nc.scalar.activation(rms[:, 0, :], ps[:, NORM_BANK, :], ACT.Sqrt,
                                     bias=eps[:, 0:1]).then_inc(rms_ready, 1)

            def activate(f, i, m):
                ft = KF * f + 2 * i + m
                act.wait_ge(gate_scaled, ft + 1)
                nc.scalar.activation(tmp_a[:, 0, :], tmp_a[:, 0, :], ACT.Silu
                                     ).then_inc(silu_ready, 1)

            def gate_up(f, i, norm=None):
                for m in range(2):
                    for c in splits_beside(m, norm):
                        split(rounds(GU0[f]) + i, c)
                    if m == 0 and norm is not None:
                        take_rms(norm)
                    activate(f, i, m)

            def down_tiles(i):
                for j in range(4):
                    for c in range(3 * j + AHEAD, 3 * j + 3 + AHEAD):
                        split(rounds(DOWN0[0]) + 3 * i, c)
                    next_norm(NORM_MIX, 4 * i + j, j % 2)

            def last_sums(dh, t):
                wait_last_tile(act, dh, t)
                if dh or t:
                    act.wait_ge(last_square, TT * dh + t)
                nc.scalar.activation(square[:, 0, :], ps[:, TT * (1 - dh) + t, :], ACT.Square,
                                     accum_out=last_sum[:, dh, t:t + 1]).then_inc(last_square, 1)

            def hi_of_cat(event):
                bank, k, g = cat_place(event)
                act.wait_ge(cat_done, CAT_EVENTS.index(event) + 1)
                nc.scalar.activation(cat_hi[:, k, :], ps[:, bank, :], ACT.Copy,
                                     scale=gain[:, g:g + 1]).then_inc(cat_hi_ready, 1)

            def hi_of_qk(h):
                own, other = DK * (h % 2), DK * ((h + 1) % 2)
                act.wait_ge(qk_ready, 3 + h // 2)
                for dst, to, tile in ((q_pair, own, h // 2), (k_pair, own, 2 + h // 2),
                                      (k_pair, other, 2 + h // 2)):
                    last = nc.scalar.activation(dst[to:to + DK, h, :], qk[own:own + DK, tile, :],
                                                ACT.Copy)
                last.then_inc(qk_hi_ready, 1)

            def group_std(h):
                act.wait_ge(var_ready, h + 1)
                nc.scalar.activation(gn_std[:], meanvar[:, :, 1], ACT.Sqrt,
                                     bias=eps[:, 1:2]).then_inc(gn_std_ready, 1)

            act.wait_ge(eps_set, 2)
            nc.scalar.activation(warm[:], eps[:, 0:1], ACT.Sqrt)

            for step, c in START:
                if step == "x":
                    if c == 0:
                        act.wait_ge(gain_landed, 16)
                    act.wait_ge(x_landed[c], 16)
                    hi_of_h(NORM_FFN[0], c)
                else:
                    landed, split_hi, part = {
                        "first": (first_landed[c], first_hi_split, slice(0, UNIT // 2)),
                        "second": (raw_landed[c], hi_split, slice(UNIT // 2, UNIT))}[step]
                    act.wait_ge(landed, 16)
                    nc.scalar.activation(w_hi[:, c, part], w_raw[:, c, part], ACT.Copy
                                         ).then_inc(split_hi, 1)
            for j in range(KD):
                first_square(j)
                if j in (3, 5):
                    split(0, j // 2 + 1)
            gate_up(0, 0, NORM_FFN[0])
            with act.Fori(1, KF // 2) as i:
                gate_up(0, i)
            for i in range(2):
                down_tiles(i)

            for n in range(MIX_UNITS):
                split(rounds(MIX0), n + AHEAD)
                if n == QK0:
                    take_rms(NORM_MIX)
                    act.wait_ge(tok_mean_done, 1)
                    nc.scalar.activation(rms_tok[:], ps[:, TOK_BANK, 0:TT], ACT.Sqrt,
                                         bias=eps[:, 0:1]).then_inc(tok_rms_ready, 1)
                if V0 <= n < G0:
                    hi_of_qk(n - V0)
                if n == V0 + 3:
                    act.wait_ge(tok_rstd_ready, 1)
                    act.wait_ge(unit_done, MIX0 + n + 1)
                    for t in range(TT):
                        nc.scalar.activation(v[:, t, :], ps[:, 4 + t, :], ACT.Copy,
                                             scale=rstd_tok[:, t:t + 1]).then_inc(v_ready, 1)
                if n == G0 + 3:
                    act.wait_ge(unit_done, MIX0 + n + 1)
                    for t in range(TT):
                        nc.scalar.activation(sg[:, t, :], ps[:, t, :], ACT.Silu,
                                             scale=rstd_tok[:, t:t + 1]).then_inc(sg_ready, 1)
                if U0 <= n < O0:
                    for task, arg in RET_TASKS[n - U0]:
                        if task == "cat":
                            hi_of_cat(arg)
                        if task == "stats":
                            group_std(arg)
                if n >= O0:
                    next_norm(NORM_FFN[1], n - O0, n % 2)

            gate_up(1, 0, NORM_FFN[1])
            with act.Fori(1, KF // 2) as i:
                gate_up(1, i)
            for c in range(2 * LAST_UNITS):
                if c == LAST_UNITS - 1:
                    for t in range(TT - 1):
                        last_sums(0, t)
                if c + AHEAD < 2 * LAST_UNITS:
                    split(rounds(DOWN0[1]), c + AHEAD)
                if c == LAST_UNITS - 1:
                    last_sums(0, TT - 1)
            nc.scalar.activation(warm[:], eps[:, 0:1], ACT.Sqrt)
            for t in range(TT):
                last_sums(1, t)
                if t == 0:
                    act.wait_ge(last_bias_ready, 1)
                act.wait_ge(last_square, TT + t + 1)
                nc.scalar.activation(rms_tok[:, t:t + 1], last_sum[:, 1, t:t + 1], ACT.Sqrt,
                                     bias=last_bias[:, t:t + 1], scale=1.0 / D
                                     ).then_inc(last_rms_ready, 1)

        @block.vector
        def _(dve):
            def split(rnd, c):
                n, s = SLOTS * rnd + c, c % SLOTS
                dve.wait_ge(hi_split, n + 1)
                nc.vector.tensor_tensor(w_lo[:, s, :], w_raw[:, s, :],
                                        w_hi[:, s, :].bitcast(F32), ALU.subtract
                                        ).then_inc(lo_split, 1)

            def lo_of_h(norm, j):
                dve.wait_ge(h_hi_ready, KD * norm + j + 1)
                nc.vector.scalar_tensor_tensor(
                    out=at(h_lo, j), in0=at(x, j),
                    scalar=gain[:, bass.ds(GAIN_NORM[norm] + j, 1)],
                    in1=at(h_hi, j).bitcast(F32), op0=ALU.mult, op1=ALU.subtract
                    ).then_inc(h_ready, 1)

            def update_x(norm, j, bank, n):
                dve.wait_ge(unit_done, n + 1)
                nc.vector.tensor_tensor(at(x, j), at(ps, bank), at(x, j), ALU.add
                                        ).then_inc(x_updated, 1)
                lo_of_h(norm, j)

            def take_rstd(norm):
                dve.wait_ge(rms_ready, norm + 1)
                nc.vector.reciprocal(rstd[:, 0, :], rms[:, 0, :]).then_inc(rstd_ready, 1)

            def activate(f, i, m):
                ft = KF * f + 2 * i + m
                n = GU0[f] + 4 * i + 2 * m
                dve.wait_ge(unit_done, n + 1)
                nc.vector.tensor_tensor(tmp_a[:, 0, :], ps[:, 2 * m, :], rstd[:, 0, :], ALU.mult
                                        ).then_inc(gate_scaled, 1)
                dve.wait_ge(unit_done, n + 2)
                if known(ft, 1):
                    dve.wait_ge(a_lo_ready, ft)
                nc.vector.scalar_tensor_tensor(out=tmp_b[:, 0, :], in0=ps[:, 2 * m + 1, :],
                                               scalar=0.5, in1=rstd[:, 0, :],
                                               op0=ALU.mult, op1=ALU.mult).then_inc(up_scaled, 1)
                dve.wait_ge(up_scaled, ft + 1)
                dve.wait_ge(silu_ready, ft + 1)
                nc.vector.tensor_tensor(at(a_hi, 2 * i + m), tmp_a[:], tmp_b[:], ALU.mult)
                nc.vector.tensor_tensor(tmp_b[:], tmp_a[:], tmp_b[:], ALU.mult).then_inc(a_ready, 1)
                dve.wait_ge(a_ready, ft + 1)
                nc.vector.tensor_tensor(at(a_lo, 2 * i + m), at(tmp_b, 0),
                                        at(a_hi, 2 * i + m).bitcast(F32), ALU.subtract
                                        ).then_inc(a_lo_ready, 1)

            def gate_up(f, i, norm=None):
                for m in range(2):
                    for c in splits_beside(m, norm):
                        split(rounds(GU0[f]) + i, c)
                    if m == 0 and norm is not None:
                        take_rstd(norm)
                        dve.wait_ge(rstd_ready, norm + 1)
                    activate(f, i, m)

            def down_tiles(i):
                for j in range(4):
                    for c in range(3 * j + AHEAD, 3 * j + 3 + AHEAD):
                        split(rounds(DOWN0[0]) + 3 * i, c)
                    update_x(NORM_MIX, 4 * i + j, 4 - 4 * i + j, DOWN0[0] + 12 * i + 3 * j + 2)

            def first_half_gains(t):
                dve.wait_ge(last_square, t + 1)
                nc.vector.tensor_tensor(x[:, t, :], ps[:, TT + t, :], rope_sb[:, 0, :], ALU.mult
                                        ).then_inc(last_gained, 1)

            def rotate(m):
                dve.wait_ge(unit_done, MIX0 + QK0 + m + 1)
                if m:
                    dve.wait_ge(qk_ready, m)
                nc.vector.tensor_tensor(rot_a[:, 0, :], ps[:, m, :], tmp_a[:, 0, :], ALU.mult)
                for src in range(0, P, DK // 2):
                    dst = src ^ (DK // 2)
                    last = nc.vector.tensor_tensor(rot_b[dst:dst + DK // 2, 0, :],
                                                   ps[src:src + DK // 2, m, :],
                                                   tmp_b[src:src + DK // 2, 0, :], ALU.mult)
                last.then_inc(rot_ready, 1)

            def lo_of_qk(h):
                own, other = DK * (h % 2), DK * ((h + 1) % 2)
                rows = slice(own, own + DK)
                dve.wait_ge(qk_hi_ready, h + 1)
                nc.vector.tensor_tensor(q_pair[other:other + DK, h, :], qk[rows, h // 2, :],
                                        q_pair[rows, h, :].bitcast(F32), ALU.subtract)
                nc.vector.tensor_tensor(k_lo[rows, h, :], qk[rows, 2 + h // 2, :],
                                        k_pair[rows, h, :].bitcast(F32), ALU.subtract
                                        ).then_inc(qk_split, 1)

            def decay_scores(h):
                dve.wait_ge(scores_done, h + 1)
                for j, (bank, col) in enumerate(SCORE_AT):
                    w = T - P * j
                    last = nc.vector.tensor_tensor(pt[:, h, PT_AT[j]:PT_AT[j] + w],
                                                   ps[:, bank, col:col + w],
                                                   decay_sb[:, h, 0:w], ALU.mult)
                last.then_inc(pt_ready, 1)

            def take_u(s):
                dve.wait_ge(unit_done, MIX0 + U0 + s + 1)
                if s >= 2:
                    dve.wait_ge(cat_done, CAT_EVENTS.index(f"y{s - 2}") + 1)
                nc.vector.tensor_tensor(u_sb[:, s % 2, :], ps[:, U_BANK[s], :], rstd[:, 0, :],
                                        ALU.mult).then_inc(u_ready, 1)

            def window_mean(s):
                w = WINDOWS[3 - s]
                levels = w.bit_length() - 1
                total = (rot_a, rot_b)[(levels - 1) % 2]
                dve.wait_ge(sum_ready, s + 1)
                nc.vector.tensor_tensor(total[:, 0, 0:16], total[:, 0, 0:16], edge_sb[:, 3 - s, :],
                                        ALU.mult).then_inc(edge_done, 1)
                dve.wait_ge(edge_done, s + 1)
                nc.vector.scalar_tensor_tensor(out=u_sb[:, s % 2, :], in0=total[:, 0, :],
                                               scalar=1.0 / w, in1=u_sb[:, s % 2, :],
                                               op0=ALU.mult, op1=ALU.subtract
                                               ).then_inc(pooled_ready, 1)

            def group_stats(h):
                dve.wait_ge(pv_done, h + 1)
                for t in range(TT):
                    last = nc.vector.bn_stats(stats[:, t, :], ps[:, h, P * t:P * (t + 1)])
                last.then_inc(stats_ready, 1)
                dve.wait_ge(stats_ready, h + 1)
                for t in range(TT):
                    last = nc.vector.bn_aggr(meanvar[:, t, :], stats[:, t, :])
                last.then_inc(var_ready, 1)

            def group_norm(h):
                dve.wait_ge(gn_std_ready, h + 1)
                nc.vector.reciprocal(gn_rstd[:], gn_std[:]).then_inc(gn_rstd_ready, 1)
                dve.wait_ge(gn_rstd_ready, h + 1)
                if h >= 2:
                    dve.wait_ge(cat_done, CAT_EVENTS.index(f"t{h - 2}") + 1)
                for t in range(TT):
                    last = nc.vector.tensor_scalar(n_sb[:, h % 2, P * t:P * (t + 1)],
                                                   ps[:, h, P * t:P * (t + 1)],
                                                   meanvar[:, t, 0:1], gn_rstd[:, t:t + 1],
                                                   ALU.subtract, ALU.mult)
                last.then_inc(gn_scaled, 1)
                dve.wait_ge(gn_scaled, h + 1)
                n3 = n_sb[:, h % 2, :].rearrange("p (t c) -> p t c", t=TT)
                nc.vector.tensor_tensor(n3, n3, sg[:, :, DV * h:DV * (h + 1)], ALU.mult
                                        ).then_inc(ret_ready, 1)

            def lo_of_cat(event):
                bank, k, g = cat_place(event)
                dve.wait_ge(cat_hi_ready, CAT_EVENTS.index(event) + 1)
                nc.vector.scalar_tensor_tensor(out=cat_lo[:, k, :], in0=ps[:, bank, :],
                                               scalar=gain[:, g:g + 1],
                                               in1=cat_hi[:, k, :].bitcast(F32),
                                               op0=ALU.mult, op1=ALU.subtract
                                               ).then_inc(cat_ready, 1)

            for step, c in START:
                if step == "x":
                    lo_of_h(NORM_FFN[0], c)
                else:
                    hi_ready, split_lo, part = {
                        "first": (first_hi_split, first_split, slice(0, UNIT // 2)),
                        "second": (hi_split, lo_split, slice(UNIT // 2, UNIT))}[step]
                    dve.wait_ge(hi_ready, c + 1)
                    nc.vector.tensor_tensor(w_lo[:, c, part], w_raw[:, c, part],
                                            w_hi[:, c, part].bitcast(F32), ALU.subtract
                                            ).then_inc(split_lo, 1)
            for j in range(3, KD, 2):
                if j > 3:
                    split(0, j // 2)
                dve.wait_ge(square_ready, j + 1)
                if j > 3:
                    dve.wait_ge(odd_added, j // 2 - 1)
                nc.vector.tensor_tensor(rms[:, 0, :], rms[:, 0, :], square[:, 1, :], ALU.add
                                        ).then_inc(odd_added, 1)
            gate_up(0, 0, NORM_FFN[0])
            with dve.Fori(1, KF // 2) as i:
                gate_up(0, i)
            with dve.Fori(0, 2) as i:
                down_tiles(i)

            for n in range(MIX_UNITS):
                split(rounds(MIX0), n + AHEAD)
                if n == QK0:
                    take_rstd(NORM_MIX)
                    dve.wait_ge(tok_rms_ready, 1)
                    nc.vector.reciprocal(rstd_tok[:], rms_tok[:]).then_inc(tok_rstd_ready, 1)
                    dve.wait_ge(rstd_ready, NORM_MIX + 1)
                    dve.wait_ge(rope_landed, 16)
                    for r, t in enumerate((tmp_a, tmp_b)):
                        nc.vector.tensor_tensor(t[:, 0, :], rope_sb[:, r, :], rstd[:, 0, :],
                                                ALU.mult).then_inc(rope_scaled, 1)
                    dve.wait_ge(rope_scaled, 2)
                if n < V0:
                    rotate(n)
                if V0 <= n < G0:
                    lo_of_qk(n - V0)
                if G0 <= n < U0:
                    if n == G0:
                        dve.wait_ge(mix_landed, 48)
                    decay_scores(n - G0)
                if U0 <= n < O0:
                    for task, arg in RET_TASKS[n - U0]:
                        {"u": take_u, "mean": window_mean, "stats": group_stats,
                         "norm": group_norm, "cat": lo_of_cat}[task](arg)
                if n >= O0:
                    update_x(NORM_FFN[1], n - O0, U_BANK[(n - O0) % 4], MIX0 + n)

            gate_up(1, 0, NORM_FFN[1])
            with dve.Fori(1, KF // 2) as i:
                gate_up(1, i)
            dve.wait_ge(last_gain_landed, 16)
            for c in range(2 * LAST_UNITS):
                if c == LAST_UNITS - 1:
                    for t in range(TT - 1):
                        first_half_gains(t)
                if c + AHEAD < 2 * LAST_UNITS:
                    split(rounds(DOWN0[1]), c + AHEAD)
                if c == LAST_UNITS - 1:
                    first_half_gains(TT - 1)
                    nc.vector.tensor_scalar(last_bias[:], last_sum[:, 0, :], 1.0 / D, RMS_EPS,
                                            ALU.mult, ALU.add).then_inc(last_bias_ready, 1)
            for t in range(TT):
                dve.wait_ge(last_rms_ready, t + 1)
                nc.vector.reciprocal(rstd_tok[:, t:t + 1], rms_tok[:, t:t + 1]
                                     ).then_inc(last_rstd_ready, 1)
                dve.wait_ge(last_rstd_ready, t + 1)
                dve.wait_ge(last_gained, t + 1)
                nc.vector.tensor_scalar(x[:, t, :], x[:, t, :], rstd_tok[:, t:t + 1], None,
                                        ALU.mult).then_inc(y_ready, 1)
                nc.vector.scalar_tensor_tensor(out=x[:, TT + t, :], in0=ps[:, t, :],
                                               scalar=rstd_tok[:, t:t + 1], in1=rope_sb[:, 1, :],
                                               op0=ALU.mult, op1=ALU.mult).then_inc(y_ready, 1)

        @block.gpsimd
        def _(pool):
            def sum_squares(norm, j, b):
                pool.wait_ge(square_ready, KD * norm + j + 1)
                pool.wait_ge(ssq_added, added(norm, j) - 1)
                nc.gpsimd.tensor_tensor(ssq[:, 0, :], ssq[:, 0, :], square[:, b, :], ALU.add
                                        ).then_inc(ssq_added, 1)

            def clear_squares(norm):
                pool.wait_ge(mean_done, norm)
                if norm == NORM_MIX + 1:
                    pool.wait_ge(tok_mean_done, 1)
                nc.gpsimd.memset(ssq[:], 0.0).then_inc(ssq_cleared, 1)
                pool.wait_ge(ssq_cleared, norm)

            def window_sums(s):
                pool.wait_ge(u_ready, s + 1)
                if s:
                    pool.wait_ge(pooled_ready, s)
                src, d, l = u_sb[:, s % 2, :], 1, 0
                while d < WINDOWS[3 - s]:
                    dst = (rot_a, rot_b)[l % 2][:, 0, :]
                    nc.gpsimd.tensor_copy(dst[:, 0:d], src[:, 0:d])
                    add = nc.gpsimd.tensor_tensor(dst[:, d:T], src[:, d:T], src[:, 0:T - d],
                                                  ALU.add)
                    src, d, l = dst, 2 * d, l + 1
                    if d < WINDOWS[3 - s]:
                        add.then_inc(sum_step, 1)
                        pool.wait_ge(sum_step, SUM_STEPS[s] + l)
                add.then_inc(sum_ready, 1)

            nc.gpsimd.memset(eps[:, 0:1], RMS_EPS).then_inc(eps_set, 1)
            nc.gpsimd.memset(eps[:, 1:2], GN_EPS).then_inc(eps_set, 1)
            nc.gpsimd.memset(mean_w[:], 1.0 / D)
            nc.gpsimd.memset(ident[:], 0.0).then_inc(setup_step, 1)
            pool.wait_ge(setup_step, 1)
            nc.gpsimd.affine_select(out=ident[:], in_=ident[:], compare_op=ALU.not_equal, fill=1.0,
                                    base=0, pattern=[[-1, P]], channel_multiplier=1
                                    ).then_inc(setup_done, 1)

            for j in range(2, KD, 2):
                pool.wait_ge(square_ready, j + 1)
                if j > 2:
                    pool.wait_ge(ssq_added, j // 2 - 1)
                nc.gpsimd.tensor_tensor(ssq[:, 0, :], ssq[:, 0, :], square[:, 0, :], ALU.add
                                        ).then_inc(ssq_added, 1)
            pool.wait_ge(ssq_added, 3)
            pool.wait_ge(odd_added, 3)
            nc.gpsimd.tensor_tensor(ssq[:, 0, :], ssq[:, 0, :], rms[:, 0, :], ALU.add
                                    ).then_inc(ssq_added, 1)
            clear_squares(NORM_MIX)
            with pool.Fori(0, KD // 2) as i:
                for b in range(2):
                    sum_squares(NORM_MIX, 2 * i + b, b)
            for m in range(4):
                pool.wait_ge(rot_ready, m + 1)
                nc.gpsimd.tensor_tensor(qk[:, m, :], rot_a[:, 0, :], rot_b[:, 0, :], ALU.add
                                        ).then_inc(qk_ready, 1)
            for s in range(4):
                window_sums(s)
            clear_squares(NORM_FFN[1])
            with pool.Fori(0, KD // 2) as i:
                for b in range(2):
                    sum_squares(NORM_FFN[1], 2 * i + b, b)


def decay_table():
    gamma = 1.0 - 2.0 ** (-5.0 - np.arange(HEADS))
    key, query = np.arange(P)[:, None], np.arange(T)[None, :]
    seen = query // CHUNK >= key // CHUNK
    dist = np.abs(query - key)
    return np.stack([np.where(seen, g ** dist, 0.0) * DK ** -0.5 for g in gamma],
                    axis=1).astype(np.float32)


def rope_table():
    half = DK // 2
    f = np.arange(P) % half
    freq = (ROPE_BASE ** (-f * 2.0 / DK)).astype(np.float32)
    ang = (np.arange(T, dtype=np.float32)[None, :] * freq[:, None]).astype(np.float64)
    sign = np.where(np.arange(P) % DK < half, 1.0, -1.0)[:, None]
    return np.stack([np.cos(ang), sign * np.sin(ang)], axis=1).astype(np.float32)


def edge_table():
    t = np.arange(16) + 1
    rows = np.stack([w / np.minimum(t, w) for w in WINDOWS])
    return np.broadcast_to(rows, (P,) + rows.shape).astype(np.float32).copy()


def kernel(**inputs):
    import concourse.bacc as bacc
    from concourse.bass_utils import run_bass_kernel_spmd

    w = {k: np.asarray(a) for k, a in inputs.items()}

    def columns(a):
        k, m = a.shape
        return np.ascontiguousarray(a.reshape(k // P, P, m // P, P).transpose(2, 1, 0, 3)
                                    .reshape(m // P, P, k))

    def k_pairs(a):
        return a.reshape(4, 2, P, T).transpose(0, 2, 1, 3).reshape(4, P, 2 * T)

    def by_feature(a):
        return a.reshape(-1, P).T

    w_in = w["w_in"][0]
    qk_cols, v_end, g_end = 2 * HEADS * DK, 2 * HEADS * DK + HEADS * DV, 2 * HEADS * (DK + DV)
    arrays = {
        "xT": np.ascontiguousarray(w["x"][0].T.reshape(KD, P, T).transpose(1, 0, 2)),
        "gate": columns(w["ffn1_gate"][0]), "up": columns(w["ffn1_up"][0]),
        "down": columns(w["ffn1_down"][0]),
        "gate2": columns(w["ffn2_gate"][0]), "up2": columns(w["ffn2_up"][0]),
        "down2": np.ascontiguousarray(w["ffn2_down"][0].reshape(LAST_UNITS, 2, P, 2, T)
                                      .transpose(3, 0, 2, 1, 4).reshape(2 * LAST_UNITS, P, UNIT)),
        "w_qku": np.concatenate([columns(w_in[:, :qk_cols]), columns(w_in[:, g_end:])]),
        "w_vg": np.concatenate([k_pairs(w_in[:, qk_cols:v_end]), k_pairs(w_in[:, v_end:g_end])]),
        "w_out": columns(w["w_out"][0]),
        "pool_w": np.ascontiguousarray(w["pool_w"][0].transpose(1, 0, 2)),
        "gains": np.ascontiguousarray(np.concatenate(
            [by_feature(a) for a in (w["norm_ffn1"], w["norm_mix"], w["norm_ffn2"],
                                     w["ret_gn_gain"], w["pool_scale"])], axis=1)),
        "last_gain": w["norm_final"],
        "decay": decay_table(), "rope": rope_table(), "edge": edge_table(),
    }
    nc = bacc.Bacc("TRN2", target_bir_lowering=False, num_devices=1)
    args = [nc.dram_tensor(f"{n}_dram", a.shape, mybir.dt.from_np(a.dtype),
                           kind="ExternalInput").ap() for n, a in arrays.items()]
    args.append(nc.dram_tensor("out_dram", (T, D), F32, kind="ExternalOutput").ap())
    program(nc, *args)
    r = run_bass_kernel_spmd(nc, [{f"{n}_dram": a for n, a in arrays.items()}], core_ids=[0])
    return r.results[0]["out_dram"][None]
```
